# Optimizing a Trainium2 kernel written in Bass

```python
import math
import jax, jax.numpy as jnp
from jax import lax
import numpy as np

D_MODEL = 2048
BATCH = 1
SEQ = 256
DEPTH = 2

HEAD_DIM = 128
A_PAIRS = ((128, 1), (512, 4), (2048, 16))
A_GROUPS = len(A_PAIRS)
A_HEADS = D_MODEL // 256
A_OUT = A_HEADS * HEAD_DIM
A_COLS = A_GROUPS * 3 * A_HEADS * HEAD_DIM
B_CHUNK = 128
B_GROUPS = D_MODEL // 256
B_WIDTH = B_GROUPS * HEAD_DIM
B_COLS = 2 * B_WIDTH
MEM_TOKENS = 256
MEM_HEADS = 4
MEM_WIDTH = MEM_HEADS * HEAD_DIM
MIX_OUT = A_OUT + MEM_WIDTH
D_FF = 4 * D_MODEL
N_LAYERS_A = (DEPTH + 1) // 2
N_LAYERS_B = DEPTH // 2
ALPHA = (2.0 * DEPTH) ** 0.25
BETA = (8.0 * DEPTH) ** -0.25
LN_EPS = 1e-5

kernel_name = "hybrid_dilated_gmlp_memory_deepnorm"

def _layer_norm(x, g, b):
    xf = x.astype(jnp.float32)
    mu = jnp.mean(xf, axis=-1, keepdims=True)
    var = jnp.mean(jnp.square(xf - mu), axis=-1, keepdims=True)
    y = (xf - mu) * lax.rsqrt(var + LN_EPS) * g.astype(jnp.float32) + b.astype(jnp.float32)
    return y.astype(x.dtype)

def _dilated_branch(q, k, v, window, dilation):
    b, s, h, dh = q.shape
    w_sub = window // dilation
    blk = w_sub
    L = s // dilation
    nb = -(-L // blk)
    Lp = nb * blk

    def to_sub(t):
        t = t.reshape(b, L, dilation, h, dh).transpose(0, 2, 1, 3, 4)
        t = jnp.pad(t, ((0, 0), (0, 0), (0, Lp - L), (0, 0), (0, 0)))
        return t.reshape(b, dilation, nb, blk, h, dh)

    qb, kb, vb = to_sub(q), to_sub(k), to_sub(v)

    def with_prev(t):
        prev = jnp.pad(t[:, :, :-1], ((0, 0), (0, 0), (1, 0), (0, 0), (0, 0), (0, 0)))
        return jnp.concatenate([prev, t], axis=3)

    kk, vv = with_prev(kb), with_prev(vb)
    scores = jnp.einsum('brnqhd,brnkhd->brnhqk', qb, kk).astype(jnp.float32) * (dh ** -0.5)
    qi = jnp.arange(blk)[:, None]
    kj = jnp.arange(2 * blk)[None, :]
    dist = qi + blk - kj
    band = (dist >= 0) & (dist <= w_sub)
    exists = (jnp.arange(nb) > 0)[:, None, None] | (kj >= blk)[None]
    mask = band[None] & exists
    scores = jnp.where(mask[None, None, :, None], scores, -jnp.inf)
    m = jnp.max(scores, axis=-1, keepdims=True)
    p = jnp.exp(scores - m)
    l = jnp.sum(p, axis=-1, keepdims=True)
    o = jnp.einsum('brnhqk,brnkhd->brnqhd', p, vv.astype(jnp.float32))
    o = o / jnp.moveaxis(l, 3, 4)
    lse = jnp.moveaxis((m + jnp.log(l))[..., 0], 3, 4)

    def from_sub(t):
        t = t.reshape((b, dilation, Lp) + t.shape[4:])[:, :, :L]
        t = jnp.moveaxis(t, 1, 2)
        return t.reshape((b, s) + t.shape[3:])

    return from_sub(o), from_sub(lse)

def _mixer_dilated(x, w_in):
    b, s, _ = x.shape
    proj = x @ w_in
    qkv = proj[..., :A_COLS].reshape(b, s, A_GROUPS, 3, A_HEADS, HEAD_DIM)
    mem_q = proj[..., A_COLS:]
    outs, lses = [], []
    for g, (window, dilation) in enumerate(A_PAIRS):
        o, lse = _dilated_branch(qkv[:, :, g, 0], qkv[:, :, g, 1], qkv[:, :, g, 2], window, dilation)
        outs.append(o)
        lses.append(lse)
    wts = jax.nn.softmax(jnp.stack(lses, axis=0), axis=0)
    o = jnp.sum(wts[..., None] * jnp.stack(outs, axis=0), axis=0)
    return o.reshape(b, s, A_OUT).astype(x.dtype), mem_q

def _mixer_gmlp(x, w_in, w_s, b_s, vnorm_g, vnorm_b):
    b, s, _ = x.shape
    proj = x @ w_in
    z = jax.nn.gelu(proj[..., :B_COLS], approximate=False)
    u, v = z[..., :B_WIDTH], z[..., B_WIDTH:]
    mem_q = proj[..., B_COLS:]
    v = _layer_norm(v, vnorm_g, vnorm_b)
    v = v.reshape(b, s // B_CHUNK, B_CHUNK, B_GROUPS, HEAD_DIM)
    causal = jnp.tril(jnp.ones((B_CHUNK, B_CHUNK), dtype=w_s.dtype))
    ws = w_s * causal[None]
    sg = jnp.einsum('gts,bcsgd->bctgd', ws, v) + b_s.T[:, :, None]
    return u * sg.reshape(b, s, B_WIDTH), mem_q

def _memory_attention(mem_q, mem, w_mem_kv):
    b, s, _ = mem_q.shape
    q = mem_q.reshape(b, s, MEM_HEADS, HEAD_DIM)
    kv = (mem @ w_mem_kv).reshape(b, MEM_TOKENS, 2, MEM_HEADS, HEAD_DIM)
    k, v = kv[:, :, 0], kv[:, :, 1]
    scores = jnp.einsum('bshd,bmhd->bhsm', q, k).astype(jnp.float32) * (HEAD_DIM ** -0.5)
    p = jax.nn.softmax(scores, axis=-1)
    o = jnp.einsum('bhsm,bmhd->bshd', p, v.astype(jnp.float32))
    return o.reshape(b, s, MEM_WIDTH).astype(mem_q.dtype)

def setup_inputs(seed: int = 0) -> dict:
    key = jax.random.key(seed)
    ks = jax.random.split(key, 20)

    def nrm(k, shape, std):
        return jax.random.normal(k, shape, jnp.float32) * std

    x = nrm(ks[0], (BATCH, SEQ, D_MODEL), 1.0)
    mem = nrm(ks[1], (BATCH, MEM_TOKENS, D_MODEL), 1.0)
    a_scale = np.ones((A_GROUPS, 3, A_HEADS * HEAD_DIM), np.float32)
    a_scale[:, 2, :] = BETA
    a_scale = jnp.asarray(np.concatenate([a_scale.reshape(-1), np.ones(MEM_WIDTH, np.float32)]))
    w_in_a = nrm(ks[2], (N_LAYERS_A, D_MODEL, A_COLS + MEM_WIDTH), D_MODEL ** -0.5) * a_scale
    b_scale = jnp.asarray(np.concatenate([np.full(B_COLS, BETA, np.float32), np.ones(MEM_WIDTH, np.float32)]))
    w_in_b = nrm(ks[3], (N_LAYERS_B, D_MODEL, B_COLS + MEM_WIDTH), D_MODEL ** -0.5) * b_scale
    w_s = nrm(ks[4], (N_LAYERS_B, B_GROUPS, B_CHUNK, B_CHUNK), B_CHUNK ** -0.5)
    b_s = 1.0 + nrm(ks[5], (N_LAYERS_B, B_GROUPS, B_CHUNK), 0.02)
    vnorm_g = 1.0 + nrm(ks[6], (N_LAYERS_B, B_WIDTH), 0.02)
    vnorm_b = nrm(ks[7], (N_LAYERS_B, B_WIDTH), 0.02)
    kv_scale = jnp.concatenate([jnp.ones((MEM_WIDTH,), jnp.float32), jnp.full((MEM_WIDTH,), BETA, jnp.float32)])
    w_mem_kv = nrm(ks[8], (DEPTH, D_MODEL, 2 * MEM_WIDTH), D_MODEL ** -0.5) * kv_scale
    w_out = nrm(ks[9], (DEPTH, MIX_OUT, D_MODEL), BETA * MIX_OUT ** -0.5)
    ln1_g = 1.0 + nrm(ks[10], (DEPTH, D_MODEL), 0.02)
    ln1_b = nrm(ks[11], (DEPTH, D_MODEL), 0.02)
    w_ff1 = nrm(ks[12], (DEPTH, D_MODEL, D_FF), BETA * D_MODEL ** -0.5)
    w_ff2 = nrm(ks[13], (DEPTH, D_FF, D_MODEL), BETA * D_FF ** -0.5)
    ln2_g = 1.0 + nrm(ks[14], (DEPTH, D_MODEL), 0.02)
    ln2_b = nrm(ks[15], (DEPTH, D_MODEL), 0.02)
    return {"x": x, "mem": mem, "w_in_a": w_in_a, "w_in_b": w_in_b, "w_s": w_s, "b_s": b_s,
            "vnorm_g": vnorm_g, "vnorm_b": vnorm_b, "w_mem_kv": w_mem_kv, "w_out": w_out,
            "ln1_g": ln1_g, "ln1_b": ln1_b, "w_ff1": w_ff1, "w_ff2": w_ff2,
            "ln2_g": ln2_g, "ln2_b": ln2_b}

def reference(x, mem, w_in_a, w_in_b, w_s, b_s, vnorm_g, vnorm_b, w_mem_kv, w_out,
              ln1_g, ln1_b, w_ff1, w_ff2, ln2_g, ln2_b):
    for i in range(DEPTH):
        j = i // 2
        if i % 2 == 0:
            mix, mem_q = _mixer_dilated(x, w_in_a[j])
        else:
            mix, mem_q = _mixer_gmlp(x, w_in_b[j], w_s[j], b_s[j], vnorm_g[j], vnorm_b[j])
        mem_o = _memory_attention(mem_q, mem, w_mem_kv[i])
        y = jnp.concatenate([mix, mem_o], axis=-1) @ w_out[i]
        x = _layer_norm(ALPHA * x + y, ln1_g[i], ln1_b[i])
        hidden = jnp.square(jax.nn.relu(x @ w_ff1[i]))
        x = _layer_norm(ALPHA * x + hidden @ w_ff2[i], ln2_g[i], ln2_b[i])
    return x


_drawn_inputs = setup_inputs


def setup_inputs(seed=0):
    import zlib

    import numpy as np

    out = dict(_drawn_inputs(seed))
    spreads = {}
    factors = {'mem': 3.893, 'b_s': 8.0, 'vnorm_g': 8.0, 'vnorm_b': 8.0, 'w_mem_kv': 3.394}
    for name, (base, spread) in spreads.items():
        noise = np.random.default_rng([zlib.crc32(name.encode()), seed]).standard_normal(out[name].shape)
        drawn = base * np.exp(spread * noise) if base else spread * noise
        out[name] = __import__('jax').numpy.asarray(drawn.astype(out[name].dtype))
    for name, factor in factors.items():
        out[name] = (out[name] * factor).astype(out[name].dtype)
    return out
```

```python
import math
from contextlib import ExitStack, contextmanager

import concourse.bass as bass
import concourse.mybir as mybir
from concourse.alu_op_type import AluOpType as ALU

F32 = mybir.dt.float32
F32R = mybir.dt.float32r
ACT = mybir.ActivationFunctionType
AXIS = mybir.AxisListType

P = 128
TOKENS = 256
D_MODEL = 2048
HALVES = TOKENS // P
HEADS = 8
GROUPS = 3
DILATION = (1, 4, 16)
WINDOW_STEPS = 128
MEM_HEADS = 4
MEM_TOKENS = 256
A_COLS = GROUPS * 3 * HEADS * P
B_WIDTH = 8 * P
D_FF = 4 * D_MODEL
DEPTH = 2
ALPHA = (2.0 * DEPTH) ** 0.25
LN_EPS = 1e-5
SCORE_SCALE = P ** -0.5
MASKED = -1e30

COLS = 512
TILES = COLS // P
K_SLAB = 2
RING = 4
AHEAD = 3
K_MODEL = D_MODEL // P
SLABS = K_MODEL // K_SLAB
MIX_TILES = HEADS + MEM_HEADS
OUT_SLABS = MIX_TILES // K_SLAB
PANELS = D_MODEL // COLS
QUARTERS = D_FF // D_MODEL
TOTAL_SLABS = (2 * DEPTH + GROUPS * 3 * 2 + 4 + DEPTH + QUARTERS * 2 * PANELS * DEPTH) * SLABS \
    + DEPTH * PANELS * OUT_SLABS


def stage(**n):
    return n


def total(*parts):
    out = {}
    for times, part in parts:
        for k, v in part.items():
            out[k] = out.get(k, 0) + times * v
    return out


COLUMNS = stage(slab=SLABS, b0=1, b1=1, b2=1, b3=1, early1=1)
ROWS_LOW = stage(slab=SLABS, b0=1, b1=1)
ROWS_HIGH = stage(slab=SLABS, b2=1, b3=1)
HIDDEN = total((1, COLUMNS), (1, stage(tmp=TILES, split=TILES, low=TILES)))
RESIDUAL = total((1, ROWS_LOW), (1, ROWS_HIGH), (1, stage(stat=2 * HALVES)))
RESIDUAL_BANKS = {k: v for k, v in RESIDUAL.items() if k != "slab"}
OUT_PAIR = total((1, RESIDUAL), (1, stage(slab=2 * (OUT_SLABS - SLABS))))
TRANSPOSE = stage(b4=2, b5=2, b6=2, b7=2, split=8, low=8)
TRANSPOSE_MIX = stage(b4=1, b5=1, b6=1, b7=1, split=4, low=4)
SCORES = stage(b4=1, b5=1, b6=1, b7=1)
ATTEND = stage(b4=TILES, b5=TILES, b6=TILES, b7=TILES, negmax=2 * TILES, exp=2 * TILES, prob=2 * TILES,
               split=TILES, step=TILES)
ATTEND_MEM = {k: v for k, v in ATTEND.items() if k != "b6"}
GATES = stage(b4=1, b5=1, b6=1, b7=1)
GROUP = total((2, COLUMNS), (1, ROWS_LOW), (1, SCORES))
HEAD_BLOCK = total((GROUPS, GROUP), (1, ATTEND))
NORM_STEPS = 7
CONSTANTS = stage(b4=1, b5=1, b6=1, b7=2)
BEFORE_LAYERS = (CONSTANTS, TRANSPOSE, TRANSPOSE, total((DEPTH, COLUMNS), (DEPTH, ROWS_LOW)), total((2, HEAD_BLOCK)))
MIXER_ENDS = ((COLUMNS, SCORES, ATTEND_MEM), (total((2, RESIDUAL)), COLUMNS, GATES, TRANSPOSE_MIX, SCORES, ATTEND_MEM))
MLP_QUARTER = total((PANELS, HIDDEN), (PANELS // 2, RESIDUAL))


class Counts:

    def __init__(self):
        self.const, self.inner = {}, {}

    def __getitem__(self, key):
        c, d = self.const.get(key, 0), self.inner.get(key)
        return c if d is None else d + c

    def passed(self, adds):
        for k, v in adds.items():
            self.const[k] = self.const.get(k, 0) + v

    @contextmanager
    def loop(self, engine, times, adds):
        const, inner = dict(self.const), dict(self.inner)
        with engine.Fori(0, times) as i:
            for k, v in adds.items():
                self.inner[k] = i * v if k not in inner else inner[k] + i * v
            yield i
            for k in set(self.const) | set(adds):
                got = self.const.get(k, 0) - const.get(k, 0)
                assert got == adds.get(k, 0), f"{k}: a turn adds {got}, not {adds.get(k, 0)}"
        self.const, self.inner = const, inner
        self.passed(total((times, adds)))


def wait(engine, semaphore, value):
    if not isinstance(value, int) or value > 0:
        engine.wait_ge(semaphore, value)


def part_full(engine, full, slab_used, c, b, columns=False):
    if columns and b == 1:
        engine.wait_ge(full[1], c["early1"] + 1)
    elif b in (0, 2):
        engine.wait_ge(full[b], c[f"b{b}"] + 1)
    else:
        engine.wait_ge(slab_used, c["slab"])


def trunk(nc, x, mem, w_in_a, w_in_b, w_s, b_s, vnorm_g, vnorm_b, w_mem_kv, w_out,
          ln1_g, ln1_b, w_ff1, w_ff2, ln2_g, ln2_b, out):
    ctx = ExitStack()
    with ctx:
        def sb(name, shape, dt=F32):
            return ctx.enter_context(nc.sbuf_tensor(name, shape, dt))

        def sem(name):
            return ctx.enter_context(nc.semaphore(name))

        raw = [sb(f"w_raw{i}", [P, K_SLAB, COLS]) for i in range(RING)]
        high = [sb(f"w_high{i}", [P, K_SLAB, COLS], F32R) for i in range(RING)]
        low = [sb(f"w_low{i}", [P, K_SLAB, COLS], F32R) for i in range(RING)]
        xT = sb("xT", [P, K_MODEL, 2, TOKENS], F32R)
        hT = sb("hT", [P, K_MODEL, 2, TOKENS], F32R)
        resid = sb("resid", [P, HALVES, D_MODEL])
        mem_kT = sb("mem_kT", [P, DEPTH, MEM_HEADS, MEM_TOKENS])
        mem_v = sb("mem_v", [P, DEPTH, HALVES, COLS])
        mask = sb("mask", [P, GROUPS, 3 * P])
        ident = sb("ident", [P, P])
        wsT = sb("wsT", [P, 8, P])
        tmp = sb("tmp", [P, TILES, TOKENS])
        vecs = sb("vecs", [P, 6 * K_MODEL + 8])
        stats = sb("stats", [P, HALVES, PANELS, 6])
        moments = sb("moments", [P, HALVES, 2])
        rstd = sb("rstd", [P, HALVES])
        shift = sb("shift", [P, HALVES])
        var = sb("var", [P, HALVES])
        root = sb("root", [P, HALVES])
        negmax = sb("negmax", [P, 2 * TILES])
        expsum = sb("expsum", [P, 2 * TILES])
        inv = sb("inv", [P, 2 * TILES])
        scores_r = sb("scores_r", [P, TILES * GROUPS * 3 * P])
        qk_r = sb("qk_r", [P, 8, TOKENS])
        v_r = sb("v_r", [P, GROUPS * HALVES * COLS])
        pt_r = sb("pt_r", [P, 2 * GROUPS * 3 * P])

        scores = scores_r[:, :].rearrange("p (h g c) -> p h g c", h=TILES, g=GROUPS)
        mem_scores = scores_r[:, 0:TILES * 2 * MEM_TOKENS].rearrange("p (h m c) -> p h m c", h=TILES, m=HALVES)
        mem_rows = scores_r[:, 0:HALVES * D_MODEL].rearrange("p (m c) -> p m c", m=HALVES)
        gain = scores_r[:, 0:D_MODEL]
        bias = scores_r[:, D_MODEL:2 * D_MODEL]
        values = v_r[:, :].rearrange("p (g m c) -> p g m c", g=GROUPS, m=HALVES)
        u = v_r[:, 0:HALVES * B_WIDTH].rearrange("p (m c) -> p m c", m=HALVES)
        v_gate = [mem_kT[:, 0, :, :].rearrange("p h c -> p (h c)"), mem_v[:, 0, :, :].rearrange("p m c -> p (m c)")]
        v_gain = pt_r[:, 0:B_WIDTH]
        v_bias = pt_r[:, B_WIDTH:2 * B_WIDTH]
        pT = [pt_r[:, i * GROUPS * 3 * P:(i + 1) * GROUPS * 3 * P] for i in range(2)]
        ws_rows = qk_r[:, 0:4, :].rearrange("p a (b s) -> p (a b) s", b=2)
        vec_rows = pt_r[:, 0:P]
        residues = tmp[:, 0:2, :]

        bank = [ctx.enter_context(nc.psum_tensor(f"bank{i}", [P, COLS], F32)) for i in range(8)]

        raw_ready = [sem(f"raw_ready{i}") for i in range(RING)]
        high_ready = sem("high_ready")
        low_ready = sem("low_ready")
        slab_used = sem("slab_used")
        full = [sem(f"full{i}") for i in range(8)]
        drained = [sem(f"drained{i}") for i in range(8)]
        tmp_ready = sem("tmp_ready")
        split_high = sem("split_high")
        split_low = sem("split_low")
        step = sem("step")
        negmax_ready = sem("negmax_ready")
        exp_ready = sem("exp_ready")
        prob_ready = sem("prob_ready")
        stats_ready = sem("stats_ready")
        var_ready = sem("var_ready")
        sqrt_ready = sem("sqrt_ready")
        norm_ready = sem("norm_ready")
        resid_ready = sem("resid_ready")
        pool_step = sem("pool_step")
        consts = sem("consts")
        residue_mask = sem("residue_mask")
        tri_ready = sem("tri_ready")
        x_in, mem_in, rows_in = sem("x_in"), sem("mem_in"), sem("rows_in")
        gain_in = sem("gain_in")
        v_gain_in = sem("v_gain_in")
        out_ready, out_done = sem("out_ready"), sem("out_done")

        block = ctx.enter_context(nc.Block())

        @block.sync
        def _(sp):
            c = Counts()

            def slabs_of(w):
                return w.rearrange("(s k p) n -> s p k n", k=K_SLAB, p=P)

            def panel(w, col, n=SLABS, first=0):
                for i in range(n):
                    slot = (c.const.get("slab", 0) + i) % RING
                    wait(sp, low_ready, c["slab"] + (i - RING + 1))
                    sp.dma_start(raw[slot][:], slabs_of(w)[first + i, :, :, bass.ds(col, COLS)]) \
                        .then_inc(raw_ready[slot], 16)
                c.passed(stage(slab=n))

            sp.dma_start(mem_rows, mem[0].rearrange("(m p) n -> p m n", p=P)).then_inc(mem_in, 16)
            sp.dma_start(resid[:], x[0].rearrange("(m p) n -> p m n", p=P)).then_inc(x_in, 16)
            for layer in range(DEPTH):
                panel(w_mem_kv[layer], 0)
                panel(w_mem_kv[layer], COLS)
            with c.loop(sp, 2, stage(slab=GROUPS * 3 * SLABS)) as b:
                with c.loop(sp, GROUPS, stage(slab=3 * SLABS)) as g:
                    for part in range(3):
                        panel(w_in_a[0], g * (3 * HEADS * P) + b * COLS + part * HEADS * P)
            panel(w_in_a[0], A_COLS)
            for layer in range(DEPTH):
                if layer == 1:
                    with c.loop(sp, 4, stage(slab=SLABS)) as p:
                        panel(w_in_b[0], p * COLS)
                    panel(w_in_b[0], 2 * B_WIDTH)
                with c.loop(sp, PANELS // 2, stage(slab=2 * OUT_SLABS)) as p:
                    panel(w_out[layer], p * (2 * COLS), OUT_SLABS)
                    panel(w_out[layer], p * (2 * COLS) + COLS, OUT_SLABS)
                with c.loop(sp, QUARTERS, stage(slab=2 * PANELS * SLABS)) as q:
                    with c.loop(sp, PANELS, stage(slab=SLABS)) as p:
                        panel(w_ff1[layer], q * D_MODEL + p * COLS)
                    with c.loop(sp, PANELS, stage(slab=SLABS)) as p:
                        for i in range(SLABS):
                            wait(sp, low_ready, c["slab"] + (i - RING + 1))
                            rows = w_ff2[layer][bass.ds(q * D_MODEL + i * K_SLAB * P, K_SLAB * P),
                                                bass.ds(p * COLS, COLS)]
                            sp.dma_start(raw[i % RING][:], rows.rearrange("(k p) n -> p k n", p=P)) \
                                .then_inc(raw_ready[i % RING], 16)
                        c.passed(stage(slab=SLABS))
            assert c["slab"] == TOTAL_SLABS
            for n in range(HALVES * PANELS):
                m, j = n // PANELS, n % PANELS
                sp.wait_ge(out_ready, n + 1)
                sp.dma_start(out[0][m * P:(m + 1) * P, j * COLS:(j + 1) * COLS],
                             resid[:, m, j * COLS:(j + 1) * COLS]).then_inc(out_done, 16)
            sp.wait_ge(out_done, 16 * HALVES * PANELS)

        @block.gpsimd
        def _(pool):
            c = Counts()
            pool.memset(ident[:], 0.0).then_inc(consts, 1)
            pool.memset(residues[:], 0.0).then_inc(consts, 1)
            pool.wait_ge(consts, 2)
            pool.affine_select(out=ident[:], in_=ident[:], compare_op=ALU.not_equal, fill=1.0, base=0,
                               pattern=[[-1, P]], channel_multiplier=1).then_inc(consts, 1)
            for g in (1, 2):
                view = residues[:, g - 1, :].rearrange("p (a b) -> p a b", b=DILATION[g])
                pool.affine_select(out=view, in_=view, compare_op=ALU.not_equal, fill=1.0, base=0,
                                   pattern=[[0, TOKENS // DILATION[g]], [-1, DILATION[g]]],
                                   channel_multiplier=1).then_inc(consts, 1)
            for i, v in enumerate((ln1_g[0], ln1_b[0], ln1_g[1], ln1_b[1], ln2_g[0], ln2_b[0])):
                pool.dma_start(vec_rows[i * K_MODEL:(i + 1) * K_MODEL, :], v.rearrange("(k p) -> k p", p=P)) \
                    .then_inc(rows_in, 16)
            pool.dma_start(vec_rows[6 * K_MODEL:6 * K_MODEL + 8, :], b_s[0]).then_inc(rows_in, 16)
            pool.dma_start(ws_rows, w_s[0].rearrange("g t s -> t g s")).then_inc(rows_in, 16)

            pool.wait_ge(residue_mask, 1)
            for g in (1, 2):
                pool.wait_ge(drained[3 + g], 1)
            for g in range(GROUPS):
                first, second = mask[:, g, 0:P], mask[:, g, P:3 * P]
                pool.affine_select(out=first, in_=first, compare_op=ALU.is_ge, fill=MASKED, base=0,
                                   pattern=[[-1, P]], channel_multiplier=1).then_inc(consts, 1)
                pool.affine_select(out=second, in_=second, compare_op=ALU.is_ge, fill=MASKED, base=P,
                                   pattern=[[-1, 2 * P]], channel_multiplier=1).then_inc(consts, 1)
            pool.wait_ge(consts, 5 + 2 * GROUPS)
            second = mask[:, 0, P:3 * P]
            pool.affine_select(out=second, in_=second, compare_op=ALU.is_ge, fill=MASKED, base=WINDOW_STEPS - P,
                               pattern=[[1, 2 * P]], channel_multiplier=-1).then_inc(consts, 1)
            pool.wait_ge(drained[7], 2)
            pool.affine_select(out=wsT[:], in_=wsT[:], compare_op=ALU.is_ge, fill=0.0, base=0,
                               pattern=[[0, 8], [1, P]], channel_multiplier=-1).then_inc(tri_ready, 1)

            pool.wait_ge(split_low, 2 * TRANSPOSE["low"])
            pool.tensor_scalar(resid[:], resid[:], ALPHA, None, ALU.mult).then_inc(resid_ready, 1)

            def stream(g_row, b_row, n):
                pool.dma_start(gain, g_row.partition_broadcast(P)).then_inc(gain_in, 16)
                pool.dma_start(bias, b_row.partition_broadcast(P)).then_inc(gain_in, 16)
                pool.wait_ge(gain_in, 32 * n)
                pool.tensor_scalar(gain, gain, ALPHA, None, ALU.mult).then_inc(pool_step, 1)
                pool.tensor_scalar(bias, bias, ALPHA, None, ALU.mult).then_inc(pool_step, 1)
                pool.wait_ge(split_low, c["low"])
                pool.wait_ge(pool_step, 4 * n - 2)
                for m in range(HALVES):
                    pool.tensor_tensor(resid[:, m, :], resid[:, m, :], gain, ALU.mult).then_inc(pool_step, 1)
                pool.wait_ge(pool_step, 4 * n)
                for m in range(HALVES):
                    last = pool.tensor_tensor(resid[:, m, :], resid[:, m, :], bias, ALU.add)
                last.then_inc(resid_ready, 1)

            for adds in BEFORE_LAYERS:
                c.passed(adds)
            for layer in range(DEPTH):
                for adds in MIXER_ENDS[layer]:
                    c.passed(adds)
                pool.wait_ge(drained[7], c["b7"])
                c.passed(TRANSPOSE)
                stream(ln1_g[layer], ln1_b[layer], 2 * layer + 1)
                pool.wait_ge(resid_ready, 2 * layer + 2)
                if layer == 0:
                    pool.dma_start(v_gain, vnorm_g[0].partition_broadcast(P)).then_inc(v_gain_in, 16)
                    pool.dma_start(v_bias, vnorm_b[0].partition_broadcast(P)).then_inc(v_gain_in, 16)
                    c.passed(total((QUARTERS, MLP_QUARTER), (1, TRANSPOSE)))
                    stream(ln2_g[layer], ln2_b[layer], 2)
                else:
                    pool.dma_start(gain, ln2_g[1].partition_broadcast(P)).then_inc(gain_in, 16)
                    pool.dma_start(bias, ln2_b[1].partition_broadcast(P)).then_inc(gain_in, 16)

        @block.scalar
        def _(act):
            c = Counts()

            def slabs(n):
                for i in range(n):
                    if isinstance(c["slab"], int) and c["slab"] + i + AHEAD >= TOTAL_SLABS:
                        break
                    slab_high(i + AHEAD)
                c.passed(stage(slab=n))

            def slab_high(i):
                at = c.const.get("slab", 0) + i
                slot = at % RING
                turns = at // RING + 1
                inner = c.inner.get("slab")
                act.wait_ge(raw_ready[slot], 16 * turns if inner is None else inner * (16 // RING) + 16 * turns)
                wait(act, slab_used, c["slab"] + (i - RING + 1))
                act.activation(high[slot][:], raw[slot][:], ACT.Copy).then_inc(high_ready, 1)

            def split(n, width, target):
                flat = tmp[:].rearrange("p a b -> p (a b)")
                for i in range(n):
                    at = i % (TILES * TOKENS // width)
                    act.wait_ge(tmp_ready, c["tmp"] + (i + 1))
                    act.activation(target(i), flat[:, at * width:(at + 1) * width], ACT.Copy) \
                        .then_inc(split_high, 1)

            def transposed(pairs, target, adds):
                for i in range(pairs):
                    j, b = i % 2, 4 + i % 4
                    act.wait_ge(drained[b], c[f"b{b}"] + (i // 4 + 1))
                    act.activation(target[:, 2 * i:2 * i + 2, 0, :], tmp[:, 2 * j:2 * j + 2, :], ACT.Copy) \
                        .then_inc(split_high, 1)
                c.passed(adds)

            def attend(first, second, nb, width, tile, adds):
                for h in range(TILES):
                    for m, part in enumerate((first(h), second(h))):
                        n = 2 * h + m
                        act.wait_ge(negmax_ready, c["negmax"] + (n + 1))
                        act.activation(part, part, ACT.Exp, bias=negmax[:, n:n + 1],
                                       accum_out=expsum[:, n:n + 1]).then_inc(exp_ready, 1)

                def head_high(h):
                    act.wait_ge(full[7], c["b7"] + (h + 1))
                    act.activation(tile(h, 0), bank[7][:, 0:TOKENS], ACT.Copy).then_inc(split_high, 1)

                for h in range(TILES):
                    for g in range(nb):
                        act.wait_ge(full[4 + g], c[f"b{4 + g}"] + (h + 1))
                        if h >= 2:
                            act.wait_ge(full[7], c["b7"] + (h - 1))
                        act.activation(pT[h % 2][:, g * width:(g + 1) * width], bank[4 + g][:, 0:width],
                                       ACT.Copy).then_inc(drained[4 + g], 1)
                    if h >= 1:
                        head_high(h - 1)
                head_high(TILES - 1)
                c.passed(adds)

            def square_root():
                act.wait_ge(var_ready, c["sqrt"] + 1)
                act.activation(root[:], var[:], ACT.Sqrt).then_inc(sqrt_ready, 1)
                c.passed(stage(sqrt=1))

            def mem_attend():
                attend(lambda h: mem_scores[:, h, 0, :], lambda h: mem_scores[:, h, 1, :], 2, TOKENS,
                       lambda h, part: hT[:, HEADS + h, part, :], ATTEND_MEM)

            c.passed(CONSTANTS)
            transposed(8, hT, TRANSPOSE)
            transposed(8, xT, TRANSPOSE)
            for i in range(AHEAD):
                slab_high(i)
            for layer in range(DEPTH):
                for adds in (COLUMNS, ROWS_LOW):
                    slabs(SLABS)
                    c.passed({k: v for k, v in adds.items() if k != "slab"})
            with c.loop(act, 2, HEAD_BLOCK) as b:
                with c.loop(act, GROUPS, GROUP):
                    for adds in (COLUMNS, COLUMNS, ROWS_LOW):
                        slabs(SLABS)
                        c.passed({k: v for k, v in adds.items() if k != "slab"})
                    c.passed(SCORES)
                attend(lambda h: scores[:, h, :, 0:P], lambda h: scores[:, h, :, P:3 * P], GROUPS, 3 * P,
                       lambda h, part: hT[:, bass.ds(b * TILES + h, 1), part, :], ATTEND)
            for layer in range(DEPTH):
                if layer == 1:
                    for part in range(2):
                        for half in range(2):
                            slabs(SLABS)
                            for m in range(HALVES):
                                b = 2 * half + m
                                part_full(act, full, slab_used, c, b)
                                cols = slice(half * COLS, (half + 1) * COLS)
                                dst = u[:, m, cols] if part == 0 else v_gate[m][:, cols]
                                act.activation(dst, bank[b][:], ACT.Gelu).then_inc(drained[b], 1)
                            c.passed({f"b{2 * half}": 1, f"b{2 * half + 1}": 1})
                slabs(SLABS // 2)
                if layer == 1:
                    square_root()
                slabs(SLABS - SLABS // 2)
                c.passed({k: v for k, v in COLUMNS.items() if k != "slab"})
                if layer == 1:
                    c.passed(GATES)
                    transposed(4, hT, TRANSPOSE_MIX)
                c.passed(SCORES)
                mem_attend()
                with c.loop(act, PANELS // 2, OUT_PAIR):
                    slabs(2 * OUT_SLABS)
                    c.passed(RESIDUAL_BANKS)
                square_root()
                transposed(8, xT, TRANSPOSE)

                def quarter(last=False):
                    with c.loop(act, PANELS, HIDDEN) as p:
                        slabs(SLABS)
                        split(TILES, TOKENS, lambda i: hT[:, bass.ds(p * TILES + i, 1), 0, :])
                        c.passed({k: v for k, v in HIDDEN.items() if k != "slab"})
                    if last:
                        for n in range(PANELS // 2):
                            slabs(2 * SLABS)
                            c.passed(RESIDUAL_BANKS)
                    else:
                        with c.loop(act, PANELS // 2, RESIDUAL):
                            slabs(2 * SLABS)
                            c.passed(RESIDUAL_BANKS)

                if layer == DEPTH - 1:
                    with c.loop(act, QUARTERS - 1, MLP_QUARTER):
                        quarter()
                    quarter(last=True)
                else:
                    with c.loop(act, QUARTERS, MLP_QUARTER):
                        quarter()
                square_root()
                if layer == 0:
                    transposed(8, xT, TRANSPOSE)

        @block.vector
        def _(dve):
            c = Counts()
            chain = [0]

            def link(instruction):
                chain[0] += 1
                instruction.then_inc(step, 1)
                dve.wait_ge(step, c["step"] + chain[0])

            def end(adds):
                assert chain[0] == adds.get("step", 0), (chain[0], adds)
                chain[0] = 0
                c.passed(adds)

            def slabs(n):
                for i in range(n):
                    if isinstance(c["slab"], int) and c["slab"] + i + AHEAD >= TOTAL_SLABS:
                        break
                    slab_low(i + AHEAD)
                c.passed(stage(slab=n))

            def slab_low(i):
                slot = (c.const.get("slab", 0) + i) % RING
                dve.wait_ge(high_ready, c["slab"] + (i + 1))
                dve.tensor_tensor(low[slot][:], raw[slot][:], high[slot][:].bitcast(F32), ALU.subtract) \
                    .then_inc(low_ready, 1)

            def fold(ct, target):
                part_full(dve, full, slab_used, c, ct, columns=True)
                return dve.tensor_reduce(target, bank[ct][:].rearrange("p (a t) -> p t a", a=2), AXIS.X, ALU.add)

            def transposed(pairs, target, adds, scale=None):
                for i in range(pairs + 1):
                    if i < pairs:
                        b, j = 4 + i % 4, i % 2
                        dve.wait_ge(full[b], c[f"b{b}"] + (i // 4 + 1))
                        wait(dve, split_low, c["low"] + max(i - 1, 0))
                        src = bank[b][:].rearrange("p (a t) -> p a t", a=2)
                        if scale is None:
                            last = dve.tensor_copy(tmp[:, 2 * j:2 * j + 2, :], src)
                        else:
                            for a in range(2):
                                k = 2 * i + a
                                last = dve.tensor_scalar(tmp[:, 2 * j + a, :], src[:, a, :],
                                                         vecs[:, scale + k:scale + k + 1],
                                                         vecs[:, scale + K_MODEL + k:scale + K_MODEL + k + 1],
                                                         ALU.mult, ALU.add)
                        last.then_inc(drained[b], 1)
                    if i >= 1:
                        j = (i - 1) % 2
                        part = target[:, 2 * i - 2:2 * i, :, :]
                        dve.wait_ge(split_high, c["split"] + i)
                        dve.tensor_tensor(part[:, :, 1, :], tmp[:, 2 * j:2 * j + 2, :],
                                          part[:, :, 0, :].bitcast(F32), ALU.subtract).then_inc(split_low, 1)
                end(adds)

            def attend(first, second, axis, tile, adds):
                for h in range(TILES):
                    for m, part in enumerate((first(h), second(h))):
                        n = 2 * h + m
                        dve.tensor_reduce(negmax[:, n:n + 1], part, axis, ALU.max, negate=True) \
                            .then_inc(negmax_ready, 1)
                for h in range(TILES):
                    dve.wait_ge(exp_ready, c["exp"] + 2 * (h + 1))
                    link(dve.reciprocal(inv[:, 2 * h:2 * h + 2], expsum[:, 2 * h:2 * h + 2]))
                    for m, part in enumerate((first(h), second(h))):
                        dve.tensor_scalar(part, part, inv[:, 2 * h + m:2 * h + m + 1], None, ALU.mult) \
                            .then_inc(prob_ready, 1)
                for h in range(TILES):
                    dve.wait_ge(split_high, c["split"] + (h + 1))
                    dve.tensor_tensor(tile(h, 1), bank[7][:, 0:TOKENS], tile(h, 0).bitcast(F32), ALU.subtract) \
                        .then_inc(drained[7], 1)
                end(adds)

            def mem_attend():
                for h in range(TILES):
                    dve.wait_ge(full[4 + h], c[f"b{4 + h}"] + 1)
                    dve.tensor_scalar(mem_scores[:, h, :, :], bank[4 + h][:].rearrange("p (m c) -> p m c", m=HALVES),
                                      SCORE_SCALE, None, ALU.mult).then_inc(drained[4 + h], 1)
                dve.wait_ge(drained[7], c["b7"] + 1)
                end(SCORES)
                attend(lambda h: mem_scores[:, h, 0, :], lambda h: mem_scores[:, h, 1, :], AXIS.X,
                       lambda h, part: hT[:, HEADS + h, part, :], ATTEND_MEM)

            def residual(p, half):
                chunk = p * 2 + half
                cols = bass.ds(p * (2 * COLS) + half * COLS, COLS)
                for m in range(HALVES):
                    b = 2 * half + m
                    part_full(dve, full, slab_used, c, b)
                    dve.tensor_tensor(resid[:, m, cols], bank[b][:], resid[:, m, cols], ALU.add) \
                        .then_inc(drained[b], 1)
                for m in range(HALVES):
                    b = 2 * half + m
                    dve.wait_ge(drained[b], c[f"b{b}"] + 1)
                    dve.bn_stats(stats[:, m, bass.ds(chunk, 1), :] if not isinstance(chunk, int) else stats[:, m, chunk, :],
                                 resid[:, m, cols]).then_inc(stats_ready, 1)
                c.passed({f"b{2 * half}": 1, f"b{2 * half + 1}": 1, "stat": HALVES})

            def normalise(source, n_stats, target):
                for m in range(HALVES):
                    last = dve.bn_aggr(moments[:, m, :], stats[:, m, 0:n_stats, :])
                link(last)
                dve.tensor_scalar(var[:], moments[:, :, 1], LN_EPS, None, ALU.add).then_inc(var_ready, 1)
                dve.wait_ge(sqrt_ready, c["sqrt"] + 1)
                link(dve.reciprocal(rstd[:], root[:]))
                link(dve.tensor_tensor(root[:], rstd[:], rstd[:], ALU.mult))
                link(dve.tensor_tensor(root[:], root[:], var[:], ALU.mult))
                link(dve.tensor_scalar(root[:], root[:], -0.5, 1.5, ALU.mult, ALU.add))
                link(dve.tensor_tensor(rstd[:], rstd[:], root[:], ALU.mult))
                link(dve.scalar_tensor_tensor(shift[:], moments[:, :, 0], -1.0, rstd[:], ALU.mult, ALU.mult))
                c.passed(stage(sqrt=1))
                for m in range(HALVES):
                    dve.tensor_scalar(target(m), source(m), rstd[:, m:m + 1], shift[:, m:m + 1],
                                      ALU.mult, ALU.add).then_inc(norm_ready, 1)

            dve.memset(mask[:, 0, :], 0.0).then_inc(residue_mask, 1)
            for g in (1, 2):
                dve.wait_ge(full[3 + g], 1)
                dve.tensor_scalar(mask[:, g, :], bank[3 + g][:, 0:3 * P], 1.0, -MASKED, ALU.subtract, ALU.mult) \
                    .then_inc(drained[3 + g], 1)
            dve.wait_ge(full[6], 1)
            dve.tensor_copy(vecs[:], bank[6][:, 0:6 * K_MODEL + 8]).then_inc(drained[6], 1)
            for half in range(2):
                dve.wait_ge(full[7], half + 1)
                dve.tensor_copy(wsT[:, 4 * half:4 * half + 4, :].rearrange("p g t -> p (g t)"), bank[7][:]) \
                    .then_inc(drained[7], 1)
            end(CONSTANTS)
            transposed(8, hT, TRANSPOSE)
            transposed(8, xT, TRANSPOSE)
            for i in range(AHEAD):
                slab_low(i)

            for layer in range(DEPTH):
                slabs(SLABS)
                for ct in range(TILES):
                    fold(ct, mem_kT[:, layer, ct, :]).then_inc(drained[ct], 1)
                end({k: v for k, v in COLUMNS.items() if k != "slab"})
                slabs(SLABS)
                for m in range(HALVES):
                    part_full(dve, full, slab_used, c, m)
                    dve.tensor_copy(mem_v[:, layer, m, :], bank[m][:]).then_inc(drained[m], 1)
                end({k: v for k, v in ROWS_LOW.items() if k != "slab"})

            dve.wait_ge(consts, 5 + 2 * GROUPS + 1)
            with c.loop(dve, 2, HEAD_BLOCK) as b:
                with c.loop(dve, GROUPS, GROUP) as g:
                    for part in range(2):
                        slabs(SLABS)
                        for ct in range(TILES):
                            fold(ct, qk_r[:, TILES * part + ct, :]).then_inc(drained[ct], 1)
                        end({k: v for k, v in COLUMNS.items() if k != "slab"})
                    slabs(SLABS)
                    for m in range(HALVES):
                        part_full(dve, full, slab_used, c, m)
                        dve.tensor_copy(values[:, bass.ds(g, 1), m, :], bank[m][:].rearrange("p (a n) -> p a n", a=1)) \
                            .then_inc(drained[m], 1)
                    end({k: v for k, v in ROWS_LOW.items() if k != "slab"})
                    for h in range(TILES):
                        dve.wait_ge(full[4 + h], c[f"b{4 + h}"] + 1)
                        dve.scalar_tensor_tensor(scores[:, h, bass.ds(g, 1), :],
                                                 bank[4 + h][:, 0:3 * P].rearrange("p (a n) -> p a n", a=1),
                                                 SCORE_SCALE, mask[:, bass.ds(g, 1), :], ALU.mult, ALU.add) \
                            .then_inc(drained[4 + h], 1)
                    end(SCORES)
                dve.wait_ge(drained[7], c["b7"])
                attend(lambda h: scores[:, h, :, 0:P], lambda h: scores[:, h, :, P:3 * P], AXIS.XY,
                       lambda h, part: hT[:, bass.ds(b * TILES + h, 1), part, :], ATTEND)

            for layer in range(DEPTH):
                if layer == 1:
                    slabs(4 * SLABS)
                    c.passed(total((2, stage(b0=1, b1=1, b2=1, b3=1))))
                slabs(SLABS // 2)
                if layer == 1:
                    for b in range(4):
                        dve.wait_ge(drained[b], c[f"b{b}"])
                    dve.wait_ge(v_gain_in, 32)
                    for m in range(HALVES):
                        for j in range(2):
                            last = dve.bn_stats(stats[:, m, j, :], v_gate[m][:, j * COLS:(j + 1) * COLS])
                            if j:
                                link(last)
                    normalise(lambda m: v_gate[m], 2, lambda m: v_gate[m])
                    c.passed(stage(xn=HALVES))
                    dve.wait_ge(norm_ready, c["xn"])
                    for m in range(HALVES):
                        link(dve.tensor_tensor(v_gate[m], v_gate[m], v_gain, ALU.mult))
                    for m in range(HALVES):
                        dve.tensor_tensor(v_gate[m], v_gate[m], v_bias, ALU.add).then_inc(norm_ready, 1)
                    c.passed(stage(xn=HALVES))
                    end(stage(step=NORM_STEPS + 2 * HALVES))
                slabs(SLABS - SLABS // 2)
                for ct in range(TILES):
                    fold(ct, qk_r[:, ct, :]).then_inc(drained[ct], 1)
                end({k: v for k, v in COLUMNS.items() if k != "slab"})
                if layer == 1:
                    for n in range(4):
                        m, half = n // 2, n % 2
                        dve.wait_ge(full[4 + n], c[f"b{4 + n}"] + 1)
                        for j in range(4):
                            g = 4 * half + j
                            cols = slice(g * P, (g + 1) * P)
                            last = dve.scalar_tensor_tensor(u[:, m, cols], bank[4 + n][:, j * P:(j + 1) * P],
                                                            vecs[:, 6 * K_MODEL + g:6 * K_MODEL + g + 1],
                                                            u[:, m, cols], ALU.add, ALU.mult)
                        last.then_inc(drained[4 + n], 1)
                    end(GATES)
                    transposed(4, hT, TRANSPOSE_MIX)
                    dve.wait_ge(resid_ready, 3)
                mem_attend()
                dve.wait_ge(resid_ready, 1 + 2 * layer)
                with c.loop(dve, PANELS // 2, OUT_PAIR) as p:
                    for half in range(2):
                        slabs(OUT_SLABS)
                        residual(p, half)
                dve.wait_ge(stats_ready, c["stat"])
                normalise(lambda m: resid[:, m, :], PANELS, lambda m: resid[:, m, :])
                c.passed(stage(xn=HALVES))
                end(stage(step=NORM_STEPS))
                transposed(8, xT, TRANSPOSE, scale=2 * K_MODEL * layer)
                def quarter(last=False):
                    with c.loop(dve, PANELS, HIDDEN) as p:
                        slabs(SLABS)
                        wait(dve, split_low, c["low"])
                        for ct in range(TILES):
                            fold(ct, tmp[:, ct, :]).then_inc(drained[ct], 1)
                        for ct in range(TILES):
                            dve.wait_ge(drained[ct], c[f"b{ct}"] + 1)
                            dve.scalar_tensor_tensor(tmp[:, ct, :], tmp[:, ct, :], 0.0, tmp[:, ct, :],
                                                     ALU.max, ALU.mult).then_inc(tmp_ready, 1)
                        for ct in range(TILES):
                            k = bass.ds(p * TILES + ct, 1)
                            dve.wait_ge(split_high, c["split"] + (ct + 1))
                            dve.tensor_tensor(hT[:, k, 1, :], tmp[:, ct:ct + 1, :], hT[:, k, 0, :].bitcast(F32),
                                              ALU.subtract).then_inc(split_low, 1)
                        end({k: v for k, v in HIDDEN.items() if k != "slab"})
                    dve.wait_ge(resid_ready, 2 + 2 * layer)
                    if last:
                        for n in range(PANELS // 2):
                            for half in range(2):
                                slabs(SLABS)
                                residual(n, half)
                    else:
                        with c.loop(dve, PANELS // 2, RESIDUAL) as p:
                            for half in range(2):
                                slabs(SLABS)
                                residual(p, half)

                if layer == DEPTH - 1:
                    with c.loop(dve, QUARTERS - 1, MLP_QUARTER):
                        quarter()
                    quarter(last=True)
                else:
                    with c.loop(dve, QUARTERS, MLP_QUARTER):
                        quarter()
                dve.wait_ge(stats_ready, c["stat"])
                normalise(lambda m: resid[:, m, :], PANELS, lambda m: resid[:, m, :])
                c.passed(stage(xn=HALVES))
                end(stage(step=NORM_STEPS))
                if layer == 0:
                    transposed(8, xT, TRANSPOSE, scale=4 * K_MODEL)
            dve.wait_ge(gain_in, 32 * 4)
            dve.wait_ge(norm_ready, c["xn"])
            for m in range(HALVES):
                for j in range(PANELS):
                    cols = slice(j * COLS, (j + 1) * COLS)
                    link(dve.tensor_tensor(resid[:, m, cols], resid[:, m, cols], gain[:, cols], ALU.mult))
                    dve.tensor_tensor(resid[:, m, cols], resid[:, m, cols], bias[:, cols], ALU.add) \
                        .then_inc(out_ready, 1)

        @block.tensor
        def _(pe):
            c = Counts()

            def passed(adds):
                c.passed(adds)

            def slab(i):
                pe.wait_ge(low_ready, c["slab"] + (i + 1))
                return (c.const.get("slab", 0) + i) % RING

            def columns_panel(acts):
                for i in range(SLABS):
                    slot = slab(i)
                    for ct in range(TILES):
                        if i == 0:
                            wait(pe, drained[ct], c[f"b{ct}"])
                        for kk in range(K_SLAB):
                            k = K_SLAB * i + kk
                            cols = slice(ct * P, (ct + 1) * P)
                            pe.matmul(bank[ct][:], high[slot][:, kk, cols], acts[:, k, :, :],
                                      start=(k == 0), stop=False)
                            last = pe.matmul(bank[ct][:, 0:TOKENS], low[slot][:, kk, cols], acts[:, k, 0, :],
                                             start=False, stop=(k == K_MODEL - 1))
                        if i == SLABS - 1 and ct < TILES - 1:
                            last.then_inc(full[ct], 1)
                    last.then_inc(slab_used, 1)
                passed(COLUMNS)

            def rows_panel(acts, half, n=SLABS):
                for i in range(n):
                    slot = slab(i)
                    for kk in range(K_SLAB):
                        k = K_SLAB * i + kk
                        for m in range(HALVES):
                            b = 2 * half + m
                            if k == 0:
                                wait(pe, drained[b], c[f"b{b}"])
                            tokens = slice(m * P, (m + 1) * P)
                            end = k == K_SLAB * n - 1
                            pe.matmul(bank[b][:], acts[:, k, 0, tokens], high[slot][:, kk, :],
                                      start=(k == 0), stop=False)
                            pe.matmul(bank[b][:], acts[:, k, 0, tokens], low[slot][:, kk, :],
                                      start=False, stop=False)
                            last = pe.matmul(bank[b][:], acts[:, k, 1, tokens], high[slot][:, kk, :],
                                             start=False, stop=end)
                            if end and m == 0:
                                last.then_inc(full[b], 1)
                    last.then_inc(slab_used, 1)
                passed({"slab": n, f"b{2 * half}": 1, f"b{2 * half + 1}": 1})

            def transpose_rows(source, pairs, adds):
                for i in range(pairs):
                    b = 4 + i % 4
                    wait(pe, drained[b], c[f"b{b}"] + i // 4)
                    for a in range(2):
                        for m in range(HALVES):
                            k = 2 * i + a
                            last = pe.transpose(bank[b][:, (2 * a + m) * P:(2 * a + m + 1) * P],
                                                source(m)[:, k * P:(k + 1) * P], ident[:])
                    last.then_inc(full[b], 1)
                passed(adds)

            def attend(parts, products, adds):
                def turn(h):
                    pe.wait_ge(prob_ready, c["prob"] + 2 * (h + 1))
                    for g, blocks in enumerate(parts(h)):
                        wait(pe, drained[4 + g], c[f"b{4 + g}"] + h)
                        for n, block in enumerate(blocks):
                            last = pe.transpose(bank[4 + g][:, n * P:(n + 1) * P], block, ident[:])
                        last.then_inc(full[4 + g], 1)

                turn(0)
                for h in range(TILES):
                    if h + 1 < TILES:
                        turn(h + 1)
                    wait(pe, drained[7], c["b7"] + h)
                    terms = products(h, pT[h % 2])
                    for g in range(len(parts(h))):
                        pe.wait_ge(drained[4 + g], c[f"b{4 + g}"] + (h + 1))
                    for n, (v, prob, tokens) in enumerate(terms):
                        last = pe.matmul(bank[7][:, tokens], v, prob, start=(n == 0), stop=(n == len(terms) - 1))
                    last.then_inc(full[7], 1)
                passed(adds)

            def mem_attend(layer):
                for h in range(TILES):
                    pe.wait_ge(drained[h], c[f"b{h}"])
                    wait(pe, drained[4 + h], c[f"b{4 + h}"])
                    for m in range(HALVES):
                        last = pe.matmul(bank[4 + h][:, m * MEM_TOKENS:(m + 1) * MEM_TOKENS],
                                         qk_r[:, h, m * P:(m + 1) * P], mem_kT[:, layer, h, :],
                                         start=True, stop=True)
                    last.then_inc(full[4 + h], 1)
                passed(SCORES)

                def parts(h):
                    return [[mem_scores[:, h, m, kt * P:(kt + 1) * P] for m in range(HALVES)] for kt in range(2)]

                def products(h, slot):
                    return [(mem_v[:, layer, kt, h * P:(h + 1) * P], slot[:, kt * TOKENS:(kt + 1) * TOKENS],
                             slice(0, TOKENS)) for kt in range(2)]

                attend(parts, products, ATTEND_MEM)

            pe.wait_ge(consts, 5)
            for g in (1, 2):
                same = residues[:, g - 1, :]
                pe.matmul(bank[3 + g][:, 0:P], same[:, 0:P], same[:, 0:P], start=True, stop=True)
                pe.matmul(bank[3 + g][:, P:3 * P], same[:, P:2 * P], same[:, :], start=True, stop=True) \
                    .then_inc(full[3 + g], 1)
            pe.wait_ge(rows_in, 16 * 8)
            n = 6 * K_MODEL + 8
            pe.transpose(bank[6][:, 0:n], vec_rows[0:n, :], ident[0:n, 0:n]).then_inc(full[6], 1)
            for half in range(2):
                wait(pe, drained[7], half)
                for j in range(4):
                    last = pe.transpose(bank[7][:, j * P:(j + 1) * P], ws_rows[:, 4 * half + j, :], ident[:])
                last.then_inc(full[7], 1)
            passed(CONSTANTS)
            pe.wait_ge(mem_in, 16)
            transpose_rows(lambda m: mem_rows[:, m, :], 8, TRANSPOSE)
            pe.wait_ge(x_in, 16)
            transpose_rows(lambda m: resid[:, m, :], 8, TRANSPOSE)

            pe.wait_ge(split_low, c["low"])
            for layer in range(DEPTH):
                columns_panel(hT)
                rows_panel(hT, 0)

            with c.loop(pe, 2, HEAD_BLOCK) as b:
                with c.loop(pe, GROUPS, GROUP) as g:
                    columns_panel(xT)
                    columns_panel(xT)
                    rows_panel(xT, 0)
                    for h in range(TILES):
                        pe.wait_ge(drained[h], c[f"b{h}"] - (1 if h < HALVES else 0))
                        wait(pe, drained[4 + h], c[f"b{4 + h}"])
                        q, k = qk_r[:, h, :], qk_r[:, TILES + h, :]
                        pe.matmul(bank[4 + h][:, 0:P], q[:, 0:P], k[:, 0:P], start=True, stop=True)
                        pe.matmul(bank[4 + h][:, P:3 * P], q[:, P:2 * P], k, start=True, stop=True) \
                            .then_inc(full[4 + h], 1)
                    passed(SCORES)

                def parts(h):
                    return [[scores[:, h, g, n * P:(n + 1) * P] for n in (0, 1, 2)] for g in range(GROUPS)]

                def products(h, slot):
                    out = []
                    for g in range(GROUPS):
                        at = g * 3 * P
                        cols = slice(h * P, (h + 1) * P)
                        out.append((values[:, g, 0, cols], slot[:, at:at + 2 * P], slice(0, TOKENS)))
                        out.append((values[:, g, 1, cols], slot[:, at + 2 * P:at + 3 * P], slice(P, TOKENS)))
                    return out

                for m in range(HALVES):
                    pe.wait_ge(drained[m], c[f"b{m}"])
                attend(parts, products, ATTEND)

            for layer in range(DEPTH):
                if layer == 1:
                    for n in range(2):
                        rows_panel(xT, 0)
                        rows_panel(xT, 1)
                columns_panel(xT)
                if layer == 1:
                    pe.wait_ge(norm_ready, c["xn"] + 2 * HALVES)
                    pe.wait_ge(tri_ready, 1)
                    for n in range(4):
                        m, half = n // 2, n % 2
                        wait(pe, drained[4 + n], c[f"b{4 + n}"])
                        for j in range(4):
                            g = 4 * half + j
                            last = pe.matmul(bank[4 + n][:, j * P:(j + 1) * P], wsT[:, g, :],
                                             v_gate[m][:, g * P:(g + 1) * P], start=True, stop=True)
                        last.then_inc(full[4 + n], 1)
                    passed(GATES)
                    passed(stage(xn=2 * HALVES))
                    for n in range(4):
                        pe.wait_ge(drained[4 + n], c[f"b{4 + n}"])
                    transpose_rows(lambda m: u[:, m, :], 4, TRANSPOSE_MIX)
                mem_attend(layer)
                pe.wait_ge(drained[7], c["b7"])
                wait(pe, split_low, c["low"])
                with c.loop(pe, PANELS // 2, OUT_PAIR):
                    rows_panel(hT, 0, OUT_SLABS)
                    rows_panel(hT, 1, OUT_SLABS)
                    passed(stage(stat=2 * HALVES))
                passed(stage(xn=HALVES))
                pe.wait_ge(norm_ready, c["xn"])
                transpose_rows(lambda m: resid[:, m, :], 8, TRANSPOSE)
                pe.wait_ge(split_low, c["low"])
                with c.loop(pe, QUARTERS, MLP_QUARTER):
                    with c.loop(pe, PANELS, HIDDEN):
                        columns_panel(xT)
                        passed({k: v for k, v in HIDDEN.items() if k not in COLUMNS})
                    with c.loop(pe, PANELS // 2, RESIDUAL):
                        pe.wait_ge(split_low, c["low"])
                        rows_panel(hT, 0)
                        rows_panel(hT, 1)
                        passed(stage(stat=2 * HALVES))
                if layer == 0:
                    passed(stage(xn=HALVES))
                    pe.wait_ge(norm_ready, c["xn"])
                    transpose_rows(lambda m: resid[:, m, :], 8, TRANSPOSE)
                    pe.wait_ge(split_low, c["low"])
            assert c["slab"] == TOTAL_SLABS


_OUT = (1, TOKENS, D_MODEL)


def kernel(**inputs):
    import numpy as np
    import concourse.bacc as bacc
    from concourse.bass_utils import run_bass_kernel_spmd

    names = ["x", "mem", "w_in_a", "w_in_b", "w_s", "b_s", "vnorm_g", "vnorm_b", "w_mem_kv", "w_out",
             "ln1_g", "ln1_b", "w_ff1", "w_ff2", "ln2_g", "ln2_b"]
    nc = bacc.Bacc("TRN2", target_bir_lowering=False, num_devices=1)
    arrays, args = {}, []
    for name in names:
        a = np.ascontiguousarray(inputs[name])
        arrays[f"in_{name}"] = a
        args.append(nc.dram_tensor(f"in_{name}", a.shape, mybir.dt.from_np(a.dtype), kind="ExternalInput").ap())
    out = nc.dram_tensor("out_0", _OUT, F32, kind="ExternalOutput").ap()
    trunk(nc, *args, out)
    r = run_bass_kernel_spmd(nc, [arrays], core_ids=[0])
    return r.results[0]["out_0"]
```

```python
import math
from contextlib import ExitStack, contextmanager

import concourse.bass as bass
import concourse.mybir as mybir
from concourse.alu_op_type import AluOpType as ALU

F32 = mybir.dt.float32
F32R = mybir.dt.float32r
ACT = mybir.ActivationFunctionType
AXIS = mybir.AxisListType

P = 128
TOKENS = 256
D_MODEL = 2048
HALVES = TOKENS // P
HEADS = 8
GROUPS = 3
DILATION = (1, 4, 16)
WINDOW_STEPS = 128
MEM_HEADS = 4
MEM_TOKENS = 256
A_COLS = GROUPS * 3 * HEADS * P
B_WIDTH = 8 * P
D_FF = 4 * D_MODEL
DEPTH = 2
ALPHA = (2.0 * DEPTH) ** 0.25
LN_EPS = 1e-5
SCORE_SCALE = P ** -0.5
MASKED = -1e30

COLS = 512
TILES = COLS // P
K_SLAB = 2
RING = 4
AHEAD = 3
K_MODEL = D_MODEL // P
SLABS = K_MODEL // K_SLAB
MIX_TILES = HEADS + MEM_HEADS
OUT_SLABS = MIX_TILES // K_SLAB
OUT_EARLY = (0, 1, 4, 5)
OUT_LATE = (2, 3)
MIX_STEPS = (2, 3)
POOL_PIECES = (1, 4)
SPATIAL_STEPS = (5, 6, 7, 7)
N_VECS = 6 * K_MODEL + 8
PANELS = D_MODEL // COLS
QUARTERS = D_FF // D_MODEL
TOTAL_SLABS = (2 * DEPTH + GROUPS * 3 * 2 + 4 + DEPTH + QUARTERS * 2 * PANELS * DEPTH) * SLABS \
    + DEPTH * PANELS * OUT_SLABS


def stage(**n):
    return n


def total(*parts):
    out = {}
    for times, part in parts:
        for k, v in part.items():
            out[k] = out.get(k, 0) + times * v
    return out


COLUMNS = stage(slab=SLABS, b0=1, b1=1, b2=1, b3=1, early1=1)
ROWS_LOW = stage(slab=SLABS, b0=1, b1=1)
HIDDEN = total((1, COLUMNS), (1, stage(tmp=TILES, split=TILES, low=TILES)))
PAIR = stage(slab=2 * SLABS, b0=1, b1=1, b2=1, b3=1)
RESIDUAL = total((1, PAIR), (1, stage(stat=2 * HALVES)))
TRANSPOSE = stage(b4=2, b5=2, b6=2, b7=2, split=8, low=8)
TRANSPOSE_MIX = stage(b4=1, b5=1, b6=1, b7=1, split=4, low=4)
CONSTANTS = stage(b4=1, b5=1, b6=1, b7=2)
SCORES = stage(b4=1, b5=1, b6=1, b7=1)
ATTEND = stage(b4=TILES, b5=TILES, b6=TILES, b7=TILES, negmax=2 * TILES, exp=2 * TILES, prob=2 * TILES,
               split=TILES)
ATTEND_MEM = {k: v for k, v in ATTEND.items() if k != "b6"}
GATES = stage(b4=1, b5=1, b6=1, b7=1)
GROUP = total((2, COLUMNS), (1, ROWS_LOW), (1, SCORES))
MLP_QUARTER = total((PANELS, HIDDEN), (PANELS // 2, RESIDUAL))
NORM = stage(xn=HALVES * PANELS)


def besides(adds, done=("slab",)):
    return {k: v for k, v in adds.items() if k not in done}


class Counts:

    def __init__(self):
        self.const, self.inner = {}, {}

    def __getitem__(self, key):
        c, d = self.const.get(key, 0), self.inner.get(key)
        return c if d is None else d + c

    def taken(self):
        keys = {f"b{i}" for i in range(8)} | {"split", "low", "negmax", "exp", "prob", "xn"} | set(self.const)
        return {k: self[k] for k in keys}

    def passed(self, adds):
        for k, v in adds.items():
            self.const[k] = self.const.get(k, 0) + v

    @contextmanager
    def loop(self, engine, times, adds):
        const, inner = dict(self.const), dict(self.inner)
        with engine.Fori(0, times) as i:
            for k, v in adds.items():
                self.inner[k] = i * v if k not in inner else inner[k] + i * v
            yield i
            for k in set(self.const) | set(adds):
                got = self.const.get(k, 0) - const.get(k, 0)
                assert got == adds.get(k, 0), f"{k}: a turn adds {got}, not {adds.get(k, 0)}"
        self.const, self.inner = const, inner
        self.passed(total((times, adds)))


def wait(engine, semaphore, value):
    if not isinstance(value, int) or value > 0:
        engine.wait_ge(semaphore, value)


def part_full(engine, full, slab_used, c, b, columns=False):
    if columns and b == 1:
        engine.wait_ge(full[1], c["early1"] + 1)
    elif b in (0, 2):
        engine.wait_ge(full[b], c[f"b{b}"] + 1)
    else:
        engine.wait_ge(slab_used, c["slab"])


def trunk(nc, x, mem, w_in_a, w_in_b, w_s, b_s, vnorm_g, vnorm_b, w_mem_kv, w_out,
          ln1_g, ln1_b, w_ff1, w_ff2, ln2_g, ln2_b, out):
    ctx = ExitStack()
    with ctx:
        def sb(name, shape, dt=F32):
            return ctx.enter_context(nc.sbuf_tensor(name, shape, dt))

        def sem(name):
            return ctx.enter_context(nc.semaphore(name))

        raw = [sb(f"w_raw{i}", [P, K_SLAB, COLS]) for i in range(RING)]
        high = [sb(f"w_high{i}", [P, K_SLAB, COLS], F32R) for i in range(RING)]
        low = [sb(f"w_low{i}", [P, K_SLAB, COLS], F32R) for i in range(RING)]
        xT = sb("xT", [P, K_MODEL, 2, TOKENS], F32R)
        hT = sb("hT", [P, K_MODEL, 2, TOKENS], F32R)
        resid = sb("resid", [P, HALVES, D_MODEL])
        mem_kT = sb("mem_kT", [P, DEPTH, MEM_HEADS, MEM_TOKENS])
        mem_v = sb("mem_v", [P, DEPTH, HALVES, COLS])
        mask = sb("mask", [P, GROUPS, 3 * P])
        ident = sb("ident", [P, P])
        wsT = sb("wsT", [P, 8, P])
        tmp = sb("tmp", [P, TILES, TOKENS])
        vecs = sb("vecs", [P, N_VECS])
        stats = sb("stats", [P, HALVES, PANELS, 6])
        moments = sb("moments", [P, HALVES, 2])
        rstd = sb("rstd", [P, HALVES])
        shift = sb("shift", [P, HALVES])
        var = sb("var", [P, HALVES])
        root = sb("root", [P, HALVES])
        warm = sb("warm", [P, 1])
        negmax = sb("negmax", [P, 2 * TILES])
        expsum = sb("expsum", [P, 2 * TILES])
        inv = sb("inv", [P, 2 * TILES])
        scores_r = sb("scores_r", [P, TILES * GROUPS * 3 * P])
        qk_r = sb("qk_r", [P, 8, TOKENS])
        v_r = sb("v_r", [P, GROUPS * HALVES * COLS])
        pt_r = sb("pt_r", [P, 2 * GROUPS * 3 * P])

        scores = scores_r[:, :].rearrange("p (h g c) -> p h g c", h=TILES, g=GROUPS)
        mem_scores = v_r[:, 0:TILES * 2 * MEM_TOKENS].rearrange("p (h m c) -> p h m c", h=TILES, m=HALVES)
        mem_rows = scores_r[:, 0:HALVES * D_MODEL].rearrange("p (m c) -> p m c", m=HALVES)
        gain = scores_r[:, 0:D_MODEL]
        bias = scores_r[:, D_MODEL:2 * D_MODEL]
        values = v_r[:, :].rearrange("p (g m c) -> p g m c", g=GROUPS, m=HALVES)
        u = v_r[:, 0:HALVES * B_WIDTH].rearrange("p (m c) -> p m c", m=HALVES)
        v_gate = [mem_kT[:, 0, :, :].rearrange("p h c -> p (h c)"), mem_v[:, 0, :, :].rearrange("p m c -> p (m c)")]
        v_gain = qk_r[:, 0:4, :].rearrange("p a t -> p (a t)")
        v_bias = qk_r[:, 4:8, :].rearrange("p a t -> p (a t)")
        pT = [pt_r[:, i * GROUPS * 3 * P:(i + 1) * GROUPS * 3 * P] for i in range(2)]
        ws_rows = qk_r[:, 0:4, :].rearrange("p a (b s) -> p (a b) s", b=2)
        vec_rows = pt_r[:, 0:P]
        residues = pt_r[:, P:P + 2 * TOKENS].rearrange("p (g t) -> p g t", g=2)

        bank = [ctx.enter_context(nc.psum_tensor(f"bank{i}", [P, COLS], F32)) for i in range(8)]

        raw_ready = [sem(f"raw_ready{i}") for i in range(RING)]
        high_ready = sem("high_ready")
        low_ready = sem("low_ready")
        slab_used = sem("slab_used")
        full = [sem(f"full{i}") for i in range(8)]
        drained = [sem(f"drained{i}") for i in range(8)]
        tmp_ready = sem("tmp_ready")
        split_high = sem("split_high")
        split_low = sem("split_low")
        step_done = sem("step_done")
        negmax_ready = sem("negmax_ready")
        exp_ready = sem("exp_ready")
        prob_ready = sem("prob_ready")
        stats_ready = sem("stats_ready")
        var_ready = sem("var_ready")
        sqrt_ready = sem("sqrt_ready")
        moments_ready = sem("moments_ready")
        norm_ready = sem("norm_ready")
        resid_ready = sem("resid_ready")
        pool_step = sem("pool_step")
        consts = sem("consts")
        window_mask = sem("window_mask")
        causal_ready = sem("causal_ready")
        x_in, rows_in = sem("x_in"), sem("rows_in")
        mem_in = [sem(f"mem_in{j}") for j in range(PANELS)]
        gain_in = sem("gain_in")
        v_gain_in = sem("v_gain_in")
        row_ready = sem("row_ready")
        out_ready = sem("out_ready")
        pool_out_ready = sem("pool_out_ready")
        out_done = sem("out_done")

        block = ctx.enter_context(nc.Block())

        @block.sync
        def _(sp):
            c = Counts()

            def slab(source):
                slot = c.const.get("slab", 0) % RING
                wait(sp, low_ready, c["slab"] + (1 - RING))
                sp.dma_start(raw[slot][:], source.rearrange("(k p) n -> p k n", p=P)).then_inc(raw_ready[slot], 16)
                c.passed(stage(slab=1))

            def panel(w, col, slabs=range(SLABS), row=0):
                for i in slabs:
                    slab(w[bass.ds(row + i * K_SLAB * P, K_SLAB * P), bass.ds(col, COLS)])

            def tokens(target, source, j, semaphore):
                cols = slice(j * COLS, (j + 1) * COLS)
                sp.dma_start(target[:, :, cols], source[0].rearrange("(m p) n -> p m n", p=P)[:, :, cols]) \
                    .then_inc(semaphore, 16)

            for j in range(PANELS):
                tokens(mem_rows, mem, j, mem_in[j])
                panel(w_mem_kv[0], 0, (j,))
            panel(w_mem_kv[0], 0, range(PANELS, SLABS))
            for j in range(PANELS):
                tokens(resid, x, j, x_in)
                panel(w_mem_kv[0], COLS, (j,))
            panel(w_mem_kv[0], COLS, range(PANELS, SLABS))
            panel(w_mem_kv[1], 0)
            panel(w_mem_kv[1], COLS)
            panel(w_in_a[0], A_COLS)
            for b in range(HEADS // TILES):
                with c.loop(sp, GROUPS, stage(slab=3 * SLABS)) as g:
                    for part in range(3):
                        panel(w_in_a[0], g * (3 * HEADS * P) + (b * COLS + part * HEADS * P))
            for layer in range(DEPTH):
                if layer == 1:
                    panel(w_in_b[0], 2 * B_WIDTH)
                    for col in (B_WIDTH, B_WIDTH + COLS, 0, COLS):
                        panel(w_in_b[0], col)
                for slabs in (OUT_EARLY, OUT_LATE):
                    for half in range(2):
                        panel(w_out[layer], half * COLS, slabs)
                for half in range(2):
                    panel(w_out[layer], (2 + half) * COLS, range(OUT_SLABS))
                with c.loop(sp, QUARTERS, stage(slab=2 * PANELS * SLABS)) as q:
                    with c.loop(sp, PANELS, stage(slab=SLABS)) as p:
                        panel(w_ff1[layer], q * D_MODEL + p * COLS)
                    with c.loop(sp, PANELS, stage(slab=SLABS)) as p:
                        panel(w_ff2[layer], p * COLS, row=q * D_MODEL)
            assert c["slab"] == TOTAL_SLABS
            for n in range(HALVES * PANELS):
                m, j = n // PANELS, n % PANELS
                if n in POOL_PIECES:
                    sp.wait_ge(pool_out_ready, POOL_PIECES.index(n) + 1)
                else:
                    sp.wait_ge(out_ready, sum(i not in POOL_PIECES for i in range(n + 1)))
                sp.dma_start(out[0][m * P:(m + 1) * P, j * COLS:(j + 1) * COLS],
                             resid[:, m, j * COLS:(j + 1) * COLS]).then_inc(out_done, 16)
            sp.wait_ge(out_done, 16 * HALVES * PANELS)

        @block.gpsimd
        def _(pool):
            c = Counts()
            pool.memset(ident[:], 0.0).then_inc(consts, 1)
            pool.memset(residues[:], 0.0).then_inc(consts, 1)
            pool.wait_ge(consts, 2)
            pool.affine_select(out=ident[:], in_=ident[:], compare_op=ALU.not_equal, fill=1.0, base=0,
                               pattern=[[-1, P]], channel_multiplier=1).then_inc(consts, 1)
            for g in (1, 2):
                view = residues[:, g - 1, :].rearrange("p (a b) -> p a b", b=DILATION[g])
                pool.affine_select(out=view, in_=view, compare_op=ALU.not_equal, fill=1.0, base=0,
                                   pattern=[[0, TOKENS // DILATION[g]], [-1, DILATION[g]]],
                                   channel_multiplier=1).then_inc(consts, 1)
            for i, v in enumerate((ln1_g[0], ln1_b[0], ln1_g[1], ln1_b[1], ln2_g[0], ln2_b[0])):
                pool.dma_start(vec_rows[i * K_MODEL:(i + 1) * K_MODEL, :], v.rearrange("(k p) -> k p", p=P)) \
                    .then_inc(rows_in, 16)
            pool.dma_start(vec_rows[6 * K_MODEL:N_VECS, :], b_s[0]).then_inc(rows_in, 16)
            pool.dma_start(ws_rows, w_s[0].rearrange("g t s -> t g s")).then_inc(rows_in, 16)

            c.passed(total((2, TRANSPOSE)))
            pool.wait_ge(window_mask, 1)
            pool.wait_ge(drained[4], c["b4"] + 1)
            pool.wait_ge(drained[5], c["b5"] + 1)
            for g in range(GROUPS):
                first, second = mask[:, g, 0:P], mask[:, g, P:3 * P]
                pool.affine_select(out=first, in_=first, compare_op=ALU.is_ge, fill=MASKED, base=0,
                                   pattern=[[-1, P]], channel_multiplier=1).then_inc(consts, 1)
                pool.affine_select(out=second, in_=second, compare_op=ALU.is_ge, fill=MASKED, base=P,
                                   pattern=[[-1, 2 * P]], channel_multiplier=1).then_inc(consts, 1)
            pool.wait_ge(consts, 5 + 2 * GROUPS)
            second = mask[:, 0, P:3 * P]
            pool.affine_select(out=second, in_=second, compare_op=ALU.is_ge, fill=MASKED, base=WINDOW_STEPS - P,
                               pattern=[[1, 2 * P]], channel_multiplier=-1).then_inc(consts, 1)
            pool.wait_ge(drained[7], c["b7"] + 2)
            pool.affine_select(out=wsT[:], in_=wsT[:], compare_op=ALU.is_ge, fill=0.0, base=0,
                               pattern=[[0, 8], [1, P]], channel_multiplier=-1).then_inc(causal_ready, 1)

            pool.wait_ge(split_low, c["low"])
            pool.tensor_scalar(resid[:], resid[:], ALPHA, None, ALU.mult).then_inc(resid_ready, 1)

            def stream(g_row, b_row, n):
                pool.dma_start(gain, g_row.partition_broadcast(P)).then_inc(gain_in, 16)
                pool.dma_start(bias, b_row.partition_broadcast(P)).then_inc(gain_in, 16)
                pool.wait_ge(gain_in, 32 * n)
                pool.tensor_scalar(gain, gain, ALPHA, None, ALU.mult).then_inc(pool_step, 1)
                pool.tensor_scalar(bias, bias, ALPHA, None, ALU.mult).then_inc(pool_step, 1)
                pool.wait_ge(split_low, c["low"])
                pool.wait_ge(pool_step, 4 * n - 2)
                for m in range(HALVES):
                    pool.tensor_tensor(resid[:, m, :], resid[:, m, :], gain, ALU.mult).then_inc(pool_step, 1)
                pool.wait_ge(pool_step, 4 * n)
                for m in range(HALVES):
                    last = pool.tensor_tensor(resid[:, m, :], resid[:, m, :], bias, ALU.add)
                last.then_inc(resid_ready, 1)

            c.passed(CONSTANTS)
            c.passed(total((1, SCORES), (1, ATTEND_MEM), (2 * GROUPS, GROUP), (2, ATTEND)))
            pool.wait_ge(drained[7], c["b7"])
            c.passed(TRANSPOSE)
            stream(ln1_g[0], ln1_b[0], 1)
            pool.wait_ge(resid_ready, 2)
            c.passed(total((QUARTERS, MLP_QUARTER), (1, TRANSPOSE)))
            stream(ln2_g[0], ln2_b[0], 2)
            c.passed(SCORES)
            pool.wait_ge(drained[7], c["b7"])
            pool.dma_start(v_gain, vnorm_g[0].partition_broadcast(P)).then_inc(v_gain_in, 16)
            pool.dma_start(v_bias, vnorm_b[0].partition_broadcast(P)).then_inc(v_gain_in, 16)
            pool.wait_ge(resid_ready, 3)
            c.passed(total((1, ATTEND_MEM), (1, TRANSPOSE_MIX), (1, TRANSPOSE)))
            stream(ln1_g[1], ln1_b[1], 3)
            pool.wait_ge(resid_ready, 4)
            pool.dma_start(gain, ln2_g[1].partition_broadcast(P)).then_inc(gain_in, 16)
            pool.dma_start(bias, ln2_b[1].partition_broadcast(P)).then_inc(gain_in, 16)
            pool.wait_ge(gain_in, 32 * 4)
            for i, n in enumerate(POOL_PIECES):
                m, j = n // PANELS, n % PANELS
                cols = slice(j * COLS, (j + 1) * COLS)
                pool.wait_ge(row_ready, n + 1)
                pool.tensor_tensor(resid[:, m, cols], resid[:, m, cols], gain[:, cols], ALU.mult).then_inc(pool_step, 1)
                pool.wait_ge(pool_step, 4 * 3 + i + 1)
                pool.tensor_tensor(resid[:, m, cols], resid[:, m, cols], bias[:, cols], ALU.add) \
                    .then_inc(pool_out_ready, 1)

        @block.scalar
        def _(act):
            c = Counts()

            def slab_high(i):
                if isinstance(c["slab"], int) and c["slab"] + i >= TOTAL_SLABS:
                    return
                at = c.const.get("slab", 0) + i
                slot, turns = at % RING, at // RING + 1
                inner = c.inner.get("slab")
                act.wait_ge(raw_ready[slot], 16 * turns if inner is None else inner * (16 // RING) + 16 * turns)
                wait(act, slab_used, c["slab"] + (i - RING + 1))
                act.activation(high[slot][:], raw[slot][:], ACT.Copy).then_inc(high_ready, 1)

            def slabs(n, before=None, between=None, first=0):
                for i in range(n):
                    if before:
                        before(first + i)
                    slab_high(AHEAD)
                    c.passed(stage(slab=1))
                    if between:
                        between(first + i)

            def pair_high(i, target, base):
                j, b = i % 2, 4 + i % 4
                act.wait_ge(drained[b], base[f"b{b}"] + (i // 4 + 1))
                act.activation(target[:, 2 * i:2 * i + 2, 0, :], tmp[:, 2 * j:2 * j + 2, :], ACT.Copy) \
                    .then_inc(split_high, 1)

            def entry_panel(target, opening=False):
                base = c.taken()

                def before(i):
                    if i + 1 < 8:
                        pair_high(i + 1, target, base)
                    if opening and i == 0:
                        slab_high(2)

                if opening:
                    slab_high(0)
                pair_high(0, target, base)
                if opening:
                    slab_high(1)
                slabs(SLABS, before=before)
                c.passed(TRANSPOSE)

            def attention(first, second, nb, width, tile):
                base = c.taken()

                def step(j):
                    if j < TILES:
                        for m, part in enumerate((first(j), second(j))):
                            n = 2 * j + m
                            act.wait_ge(negmax_ready, base["negmax"] + (n + 1))
                            act.activation(part, part, ACT.Exp, bias=negmax[:, n:n + 1],
                                           accum_out=expsum[:, n:n + 1]).then_inc(exp_ready, 1)
                    h = j - 2
                    if 0 <= h < TILES:
                        for g in range(nb):
                            act.wait_ge(full[4 + g], base[f"b{4 + g}"] + (h + 1))
                            if h >= 2:
                                act.wait_ge(full[7], base["b7"] + (h - 1))
                            act.activation(pT[h % 2][:, g * width:(g + 1) * width], bank[4 + g][:, 0:width],
                                           ACT.Copy).then_inc(drained[4 + g], 1)
                    h = j - 3
                    if 0 <= h < TILES:
                        act.wait_ge(full[7], base["b7"] + (h + 1))
                        act.activation(tile(h, 0), bank[7][:, 0:TOKENS], ACT.Copy).then_inc(split_high, 1)

                return step

            def mem_attention():
                return attention(lambda h: mem_scores[:, h, 0, :], lambda h: mem_scores[:, h, 1, :], 2, TOKENS,
                                 lambda h, part: hT[:, HEADS + h, part, :])

            def block_attention(b):
                return attention(lambda h: scores[:, h, :, 0:P], lambda h: scores[:, h, :, P:3 * P], GROUPS, 3 * P,
                                 lambda h, part: hT[:, b * TILES + h, part, :])

            def square_root():
                act.activation(warm[:], ident[:, 0:1], ACT.Sqrt)
                act.wait_ge(var_ready, c["sqrt"] + 1)
                act.activation(root[:], var[:], ACT.Sqrt).then_inc(sqrt_ready, 1)
                c.passed(stage(sqrt=1))

            def gelu(target, half):
                for m in range(HALVES):
                    b = 2 * half + m
                    part_full(act, full, slab_used, c, b)
                    act.activation(target(m)[:, half * COLS:(half + 1) * COLS], bank[b][:], ACT.Gelu) \
                        .then_inc(drained[b], 1)
                c.passed({f"b{2 * half}": 1, f"b{2 * half + 1}": 1})

            entry_panel(hT, opening=True)
            c.passed(besides(COLUMNS))
            base = c.taken()
            slabs(SLABS, before=lambda i: i and pair_high(i - 1, xT, base))
            pair_high(SLABS - 1, xT, base)
            c.passed(TRANSPOSE)
            c.passed(besides(ROWS_LOW))
            slabs(SLABS)
            c.passed(besides(COLUMNS))
            c.passed(CONSTANTS)
            slabs(SLABS)
            c.passed(besides(ROWS_LOW))

            slabs(SLABS)
            c.passed(besides(COLUMNS))
            c.passed(SCORES)
            pending, adds = mem_attention(), ATTEND_MEM
            for b in range(HEADS // TILES):
                slabs(SLABS, between=pending)
                c.passed(adds)
                c.passed(besides(COLUMNS))
                slabs(2 * SLABS)
                c.passed(besides(total((1, COLUMNS), (1, ROWS_LOW), (1, SCORES))))
                with c.loop(act, GROUPS - 1, GROUP):
                    slabs(3 * SLABS)
                    c.passed(besides(GROUP))
                pending, adds = block_attention(b), ATTEND
            for layer in range(DEPTH):
                if layer == 1:
                    entry_panel(xT)
                    c.passed(besides(COLUMNS))
                    c.passed(SCORES)
                    step = mem_attention()
                    slabs(SLABS, between=step)
                    gelu(lambda m: v_gate[m], 0)
                    c.passed(ATTEND_MEM)
                    slabs(SLABS)
                    gelu(lambda m: v_gate[m], 1)
                    slabs(SLABS, between=lambda i: i == 0 and square_root())
                    gelu(lambda m: u[:, m, :], 0)
                    c.passed(GATES)
                    base = c.taken()
                    slabs(SLABS, between=lambda i: i in MIX_STEPS and pair_high(MIX_STEPS.index(i), hT, base))
                    gelu(lambda m: u[:, m, :], 1)
                    pending = lambda i: i in MIX_STEPS and pair_high(2 + MIX_STEPS.index(i), hT, base)
                    adds = TRANSPOSE_MIX
                slabs(2 * len(OUT_EARLY), between=pending)
                c.passed(adds)
                slabs(2 * OUT_SLABS - 2 * len(OUT_EARLY) + 2 * OUT_SLABS)
                c.passed(besides(total((2, RESIDUAL))))
                square_root()
                entry_panel(xT)

                def hidden(p):
                    for ct in range(TILES):
                        act.wait_ge(tmp_ready, c["tmp"] + (ct + 1))
                        act.activation(hT[:, bass.ds(p * TILES + ct, 1), 0, :], tmp[:, ct:ct + 1, :], ACT.Copy) \
                            .then_inc(split_high, 1)
                    c.passed(besides(HIDDEN))

                def rest(n, last=False):
                    with c.loop(act, n, HIDDEN) as p:
                        slabs(SLABS)
                        hidden(p + (PANELS - n))
                    if last:
                        slabs(PANELS * SLABS)
                        c.passed(besides(total((PANELS // 2, RESIDUAL))))
                    else:
                        with c.loop(act, PANELS // 2, RESIDUAL):
                            slabs(2 * SLABS)
                            c.passed(besides(RESIDUAL))

                hidden(0)
                rest(PANELS - 1)
                with c.loop(act, QUARTERS - 1 if layer == 0 else QUARTERS - 2, MLP_QUARTER):
                    rest(PANELS)
                if layer == 1:
                    rest(PANELS, last=True)
                square_root()
            act.wait_ge(moments_ready, 1)
            for m in range(HALVES):
                for j in range(PANELS):
                    cols = slice(j * COLS, (j + 1) * COLS)
                    act.activation(resid[:, m, cols], resid[:, m, cols], ACT.Identity, bias=shift[:, m:m + 1],
                                   scale=rstd[:, m:m + 1]).then_inc(row_ready, 1)

        @block.vector
        def _(dve):
            c = Counts()

            def link(instruction):
                c.passed(stage(step=1))
                instruction.then_inc(step_done, 1)
                dve.wait_ge(step_done, c["step"])

            def slab_low(i):
                if isinstance(c["slab"], int) and c["slab"] + i >= TOTAL_SLABS:
                    return
                slot = (c.const.get("slab", 0) + i) % RING
                dve.wait_ge(high_ready, c["slab"] + (i + 1))
                dve.tensor_tensor(low[slot][:], raw[slot][:], high[slot][:].bitcast(F32), ALU.subtract) \
                    .then_inc(low_ready, 1)

            def slabs(n, before=None, between=None, first=0):
                for i in range(n):
                    if before:
                        before(first + i)
                    slab_low(AHEAD)
                    c.passed(stage(slab=1))
                    if between:
                        between(first + i)

            def columns(target, before=None, between=None, free=None):
                slabs(SLABS - 1, before, between)
                if before:
                    before(SLABS - 1)
                c.passed(stage(slab=1))
                if free:
                    free()
                for ct in range(TILES):
                    part_full(dve, full, slab_used, c, ct, columns=True)
                    dve.tensor_reduce(target(ct), bank[ct][:].rearrange("p (a t) -> p t a", a=2), AXIS.X, ALU.add) \
                        .then_inc(drained[ct], 1)
                slab_low(AHEAD - 1)
                if between:
                    between(SLABS - 1)

            def take(i, base, scale=None):
                b, j = 4 + i % 4, i % 2
                dve.wait_ge(full[b], base[f"b{b}"] + (i // 4 + 1))
                wait(dve, split_low, base["low"] + max(i - 1, 0))
                src = bank[b][:].rearrange("p (a t) -> p a t", a=2)
                if scale is None:
                    last = dve.tensor_copy(tmp[:, 2 * j:2 * j + 2, :], src)
                else:
                    for a in range(2):
                        k = 2 * i + a
                        last = dve.tensor_scalar(tmp[:, 2 * j + a, :], src[:, a, :],
                                                 vecs[:, scale + k:scale + k + 1],
                                                 vecs[:, scale + K_MODEL + k:scale + K_MODEL + k + 1],
                                                 ALU.mult, ALU.add)
                last.then_inc(drained[b], 1)

            def pair_low(i, target, base):
                j, part = i % 2, target[:, 2 * i:2 * i + 2, :, :]
                dve.wait_ge(split_high, base["split"] + (i + 1))
                dve.tensor_tensor(part[:, :, 1, :], tmp[:, 2 * j:2 * j + 2, :],
                                  part[:, :, 0, :].bitcast(F32), ALU.subtract).then_inc(split_low, 1)

            def entry_panel(acts, target, scale=None, free=None, opening=False):
                base = c.taken()
                if not opening:
                    dve.wait_ge(stats_ready, c["stat"])
                    moments_of(PANELS)
                    normalise(0)
                    normalise(1)
                take(0, base, scale)
                take(1, base, scale)
                if opening:
                    slab_low(0)
                pair_low(0, acts, base)
                if opening:
                    slab_low(1)

                def before(i):
                    if i + 2 < 8:
                        take(i + 2, base, scale)
                    if i + 1 < 8:
                        pair_low(i + 1, acts, base)
                    if i == 0:
                        slab_low(AHEAD - 1)
                    if not opening and i + 2 < PANELS:
                        normalise(i + 2)

                columns(target, before=before, free=free)
                c.passed(TRANSPOSE)
                if not opening:
                    c.passed(NORM)

            def attention(first, second, axis, tile):
                base = c.taken()

                def maxima(h):
                    for m, part in enumerate((first(h), second(h))):
                        n = 2 * h + m
                        dve.tensor_reduce(negmax[:, n:n + 1], part, axis, ALU.max, negate=True) \
                            .then_inc(negmax_ready, 1)

                def step(j):
                    if 0 <= j - 1 < TILES:
                        h = j - 1
                        dve.wait_ge(exp_ready, base["exp"] + 2 * (h + 1))
                        link(dve.reciprocal(inv[:, 2 * h:2 * h + 2], expsum[:, 2 * h:2 * h + 2]))
                        for m, part in enumerate((first(h), second(h))):
                            dve.tensor_scalar(part, part, inv[:, 2 * h + m:2 * h + m + 1], None, ALU.mult) \
                                .then_inc(prob_ready, 1)
                    if j + 1 < TILES:
                        maxima(j + 1)
                    h = j - 3
                    if 0 <= h < TILES:
                        dve.wait_ge(split_high, base["split"] + (h + 1))
                        dve.tensor_tensor(tile(h, 1), bank[7][:, 0:TOKENS], tile(h, 0).bitcast(F32), ALU.subtract) \
                            .then_inc(drained[7], 1)

                maxima(0)
                return step

            def mem_attention():
                return attention(lambda h: mem_scores[:, h, 0, :], lambda h: mem_scores[:, h, 1, :], AXIS.X,
                                 lambda h, part: hT[:, HEADS + h, part, :])

            def block_attention(b):
                return attention(lambda h: scores[:, h, :, 0:P], lambda h: scores[:, h, :, P:3 * P], AXIS.XY,
                                 lambda h, part: hT[:, b * TILES + h, part, :])

            def take_mem_scores():
                for h in range(TILES):
                    dve.wait_ge(full[4 + h], c[f"b{4 + h}"] + 1)
                    dve.tensor_scalar(mem_scores[:, h, :, :], bank[4 + h][:].rearrange("p (m c) -> p m c", m=HALVES),
                                      SCORE_SCALE, None, ALU.mult).then_inc(drained[4 + h], 1)
                c.passed(SCORES)
                dve.wait_ge(drained[7], c["b7"])

            def residual(chunk, half):
                cols = bass.ds(chunk * COLS, COLS)
                for m in range(HALVES):
                    b = 2 * half + m
                    part_full(dve, full, slab_used, c, b)
                    dve.tensor_tensor(resid[:, m, cols], bank[b][:], resid[:, m, cols], ALU.add) \
                        .then_inc(drained[b], 1)
                    dve.wait_ge(drained[b], c[f"b{b}"] + 1)
                    dve.bn_stats(stats[:, m, bass.ds(chunk, 1), :], resid[:, m, cols]).then_inc(stats_ready, 1)
                c.passed({f"b{2 * half}": 1, f"b{2 * half + 1}": 1, "stat": HALVES})

            def moments_of(n_stats, ready=None):
                for m in range(HALVES):
                    last = dve.bn_aggr(moments[:, m, :], stats[:, m, 0:n_stats, :])
                link(last)
                dve.tensor_scalar(var[:], moments[:, :, 1], LN_EPS, None, ALU.add).then_inc(var_ready, 1)
                dve.wait_ge(sqrt_ready, c["sqrt"] + 1)
                link(dve.reciprocal(rstd[:], root[:]))
                link(dve.tensor_tensor(root[:], rstd[:], rstd[:], ALU.mult))
                link(dve.tensor_tensor(root[:], root[:], var[:], ALU.mult))
                link(dve.tensor_scalar(root[:], root[:], -0.5, 1.5, ALU.mult, ALU.add))
                link(dve.tensor_tensor(rstd[:], rstd[:], root[:], ALU.mult))
                last = dve.scalar_tensor_tensor(shift[:], moments[:, :, 0], -1.0, rstd[:], ALU.mult, ALU.mult)
                if ready is None:
                    link(last)
                else:
                    last.then_inc(ready, 1)
                c.passed(stage(sqrt=1))

            def last_residual(n_slabs, chunk, half):
                slabs(n_slabs - 1)
                c.passed(stage(slab=1))
                residual(chunk, half)

            def normalise(j):
                cols = slice(j * COLS, (j + 1) * COLS)
                for m in range(HALVES):
                    dve.tensor_scalar(resid[:, m, cols], resid[:, m, cols], rstd[:, m:m + 1],
                                      shift[:, m:m + 1], ALU.mult, ALU.add).then_inc(norm_ready, 1)

            entry_panel(hT, lambda ct: mem_kT[:, 0, ct, :], opening=True)
            c.passed(besides(COLUMNS))

            def take_values(target):
                for m in range(HALVES):
                    part_full(dve, full, slab_used, c, m)
                    dve.tensor_copy(target(m), bank[m][:]).then_inc(drained[m], 1)
                c.passed(besides(ROWS_LOW))

            base = c.taken()

            def split_x(i):
                take(i, base)
                if i:
                    pair_low(i - 1, xT, base)

            slabs(SLABS, before=split_x)
            take_values(lambda m: mem_v[:, 0, m, :])
            pair_low(SLABS - 1, xT, base)
            c.passed(TRANSPOSE)

            base = c.taken()

            def constants(i):
                if i == 1:
                    dve.memset(mask[:, 0, :], 0.0).then_inc(window_mask, 1)
                    for g in (1, 2):
                        b = 3 + g
                        dve.wait_ge(full[b], base[f"b{b}"] + 1)
                        dve.tensor_scalar(mask[:, g, :], bank[b][:, 0:3 * P], 1.0, -MASKED, ALU.subtract, ALU.mult) \
                            .then_inc(drained[b], 1)
                    dve.wait_ge(full[6], base["b6"] + 1)
                    dve.tensor_copy(vecs[:], bank[6][:, 0:N_VECS]).then_inc(drained[6], 1)
                if i in (1, 2):
                    half = i - 1
                    dve.wait_ge(full[7], base["b7"] + (half + 1))
                    dve.tensor_copy(wsT[:, 4 * half:4 * half + 4, :].rearrange("p g t -> p (g t)"), bank[7][:]) \
                        .then_inc(drained[7], 1)

            columns(lambda ct: mem_kT[:, 1, ct, :], between=constants)
            c.passed(besides(COLUMNS))
            c.passed(CONSTANTS)
            slabs(SLABS)
            take_values(lambda m: mem_v[:, 1, m, :])

            def projected(first, between=None):
                columns(lambda ct: qk_r[:, first + ct, :], between=between)
                c.passed(besides(COLUMNS))

            def group(g, between=None):
                projected(0, between)
                if between:
                    c.passed(adds)
                projected(TILES)
                slabs(SLABS)
                for m in range(HALVES):
                    part_full(dve, full, slab_used, c, m)
                    dve.tensor_copy(values[:, bass.ds(g, 1), m, :], bank[m][:].rearrange("p (a n) -> p a n", a=1)) \
                        .then_inc(drained[m], 1)
                c.passed(besides(ROWS_LOW))
                for h in range(TILES):
                    dve.wait_ge(full[4 + h], c[f"b{4 + h}"] + 1)
                    dve.scalar_tensor_tensor(scores[:, h, bass.ds(g, 1), :],
                                             bank[4 + h][:, 0:3 * P].rearrange("p (a n) -> p a n", a=1),
                                             SCORE_SCALE, mask[:, bass.ds(g, 1), :], ALU.mult, ALU.add) \
                        .then_inc(drained[4 + h], 1)
                c.passed(SCORES)

            projected(0)
            take_mem_scores()
            dve.wait_ge(consts, 5 + 2 * GROUPS + 1)
            pending, adds = mem_attention(), ATTEND_MEM
            for b in range(HEADS // TILES):
                group(0, pending)
                with c.loop(dve, GROUPS - 1, GROUP) as i:
                    group(i + 1)
                dve.wait_ge(drained[7], c["b7"])
                pending, adds = block_attention(b), ATTEND

            for layer in range(DEPTH):
                if layer == 1:
                    entry_panel(xT, lambda ct: qk_r[:, ct, :], scale=4 * K_MODEL)
                    c.passed(besides(COLUMNS))
                    take_mem_scores()
                    v_base = c.taken()
                    slabs(SLABS, between=mem_attention())
                    c.passed(ATTEND_MEM)

                    def gate_stats(half):
                        for m in range(HALVES):
                            b = 2 * half + m
                            dve.wait_ge(drained[b], v_base[f"b{b}"] + 1)
                            last = dve.bn_stats(stats[:, m, half, :], v_gate[m][:, half * COLS:(half + 1) * COLS])
                        return last

                    slabs(SLABS, between=lambda i: i == 0 and gate_stats(0))
                    c.passed(besides(PAIR))

                    def gate_norm(i):
                        if i == 0:
                            link(gate_stats(1))
                            moments_of(2)
                        if i == 1:
                            dve.wait_ge(v_gain_in, 32)
                            for m in range(HALVES):
                                last = dve.tensor_scalar(v_gate[m], v_gate[m], rstd[:, m:m + 1],
                                                         shift[:, m:m + 1], ALU.mult, ALU.add)
                            link(last)
                        if i == 2:
                            for m in range(HALVES):
                                last = dve.tensor_tensor(v_gate[m], v_gate[m], v_gain, ALU.mult)
                            link(last)
                        if i == 3:
                            for m in range(HALVES):
                                dve.tensor_tensor(v_gate[m], v_gate[m], v_bias, ALU.add).then_inc(norm_ready, 1)

                    def gate(half):
                        for m in range(HALVES):
                            dve.wait_ge(drained[2 * half + m], c[f"b{2 * half + m}"] + 1)
                            b = 4 + 2 * half + m
                            dve.wait_ge(full[b], gates[f"b{b}"] + 1)
                            for j in range(4):
                                g = 4 * half + j
                                cols = slice(g * P, (g + 1) * P)
                                last = dve.scalar_tensor_tensor(u[:, m, cols], bank[b][:, j * P:(j + 1) * P],
                                                                vecs[:, 6 * K_MODEL + g:6 * K_MODEL + g + 1],
                                                                u[:, m, cols], ALU.add, ALU.mult)
                            last.then_inc(drained[b], 1)

                    gates = c.taken()
                    slabs(SLABS, between=gate_norm)
                    c.passed(stage(xn=HALVES))
                    gate(0)
                    c.passed(GATES)
                    base = c.taken()

                    def split_mix(i, first=0):
                        if i in MIX_STEPS:
                            pair = first + MIX_STEPS.index(i)
                            take(pair, base)
                            pair_low(pair, hT, base)

                    slabs(SLABS, between=split_mix)
                    gate(1)
                    c.passed(besides(PAIR))
                    pending, adds = (lambda i: split_mix(i, 2)), TRANSPOSE_MIX
                dve.wait_ge(resid_ready, 1 + 2 * layer)
                slabs(2 * len(OUT_EARLY), between=pending)
                c.passed(adds)
                for half in range(2):
                    slabs(len(OUT_LATE))
                    residual(half, half)
                slabs(OUT_SLABS)
                residual(2, 0)
                last_residual(OUT_SLABS, 3, 1)
                low_base = c["low"] + 8
                entry_panel(xT, lambda ct: tmp[:, ct, :], scale=2 * K_MODEL * layer,
                            free=lambda: dve.wait_ge(split_low, low_base))

                def hidden(p):
                    for ct in range(TILES):
                        dve.wait_ge(drained[ct], c[f"b{ct}"] + 1)
                        dve.scalar_tensor_tensor(tmp[:, ct, :], tmp[:, ct, :], 0.0, tmp[:, ct, :],
                                                 ALU.max, ALU.mult).then_inc(tmp_ready, 1)
                    for ct in range(TILES):
                        k = bass.ds(p * TILES + ct, 1)
                        dve.wait_ge(split_high, c["split"] + (ct + 1))
                        dve.tensor_tensor(hT[:, k, 1, :], tmp[:, ct:ct + 1, :], hT[:, k, 0, :].bitcast(F32),
                                          ALU.subtract).then_inc(split_low, 1)
                    c.passed(besides(HIDDEN))

                def rest(n, last=False):
                    with c.loop(dve, n, HIDDEN) as p:
                        columns(lambda ct: tmp[:, ct, :], free=lambda: dve.wait_ge(split_low, c["low"]))
                        hidden(p + (PANELS - n))
                    dve.wait_ge(resid_ready, 2 + 2 * layer)
                    if last:
                        for chunk in range(PANELS - 1):
                            slabs(SLABS)
                            residual(chunk, chunk % 2)
                        last_residual(SLABS, PANELS - 1, (PANELS - 1) % 2)
                    else:
                        with c.loop(dve, PANELS // 2, RESIDUAL) as p:
                            for half in range(2):
                                slabs(SLABS)
                                residual(p * 2 + half, half)

                hidden(0)
                rest(PANELS - 1)
                with c.loop(dve, QUARTERS - 2, MLP_QUARTER):
                    rest(PANELS)
                rest(PANELS, last=True)

            dve.wait_ge(stats_ready, c["stat"])
            moments_of(PANELS, moments_ready)
            dve.wait_ge(gain_in, 32 * 4)
            for n in (n for n in range(HALVES * PANELS) if n not in POOL_PIECES):
                m, j = n // PANELS, n % PANELS
                cols = slice(j * COLS, (j + 1) * COLS)
                dve.wait_ge(row_ready, n + 1)
                link(dve.tensor_tensor(resid[:, m, cols], resid[:, m, cols], gain[:, cols], ALU.mult))
                dve.tensor_tensor(resid[:, m, cols], resid[:, m, cols], bias[:, cols], ALU.add) \
                    .then_inc(out_ready, 1)

        @block.tensor
        def _(pe):
            c = Counts()

            def next_slab():
                pe.wait_ge(low_ready, c["slab"] + 1)
                return c.const.get("slab", 0) % RING

            def columns_panel(acts, before=None, between=None):
                banks = c.taken()
                for i in range(SLABS):
                    if before:
                        before(i)
                    slot = next_slab()
                    for ct in range(TILES):
                        if i == 0:
                            wait(pe, drained[ct], banks[f"b{ct}"])
                        for kk in range(K_SLAB):
                            k = K_SLAB * i + kk
                            cols = slice(ct * P, (ct + 1) * P)
                            pe.matmul(bank[ct][:], high[slot][:, kk, cols], acts[:, k, :, :],
                                      start=(k == 0), stop=False)
                            last = pe.matmul(bank[ct][:, 0:TOKENS], low[slot][:, kk, cols], acts[:, k, 0, :],
                                             start=False, stop=(k == K_MODEL - 1))
                        if i == SLABS - 1 and ct < TILES - 1:
                            last.then_inc(full[ct], 1)
                    last.then_inc(slab_used, 1)
                    c.passed(stage(slab=1))
                    if between:
                        between(i)
                c.passed(besides(COLUMNS))

            def rows_slabs(acts, half, slabs, start=True, stop=True, before=None, between=None, first=0):
                slabs = list(slabs)
                for n, i in enumerate(slabs):
                    if before:
                        before(n)
                    slot = next_slab()
                    for m in range(HALVES):
                        for kk in range(K_SLAB):
                            k = K_SLAB * i + kk
                            b = 2 * half + m
                            opens = start and n == 0 and kk == 0
                            closes = stop and n == len(slabs) - 1 and kk == K_SLAB - 1
                            if opens:
                                wait(pe, drained[b], c[f"b{b}"])
                            tokens = slice(m * P, (m + 1) * P)
                            pe.matmul(bank[b][:], acts[:, k, 0, tokens], high[slot][:, kk, :],
                                      start=opens, stop=False)
                            pe.matmul(bank[b][:], acts[:, k, 0, tokens], low[slot][:, kk, :],
                                      start=False, stop=False)
                            last = pe.matmul(bank[b][:], acts[:, k, 1, tokens], high[slot][:, kk, :],
                                             start=False, stop=closes)
                            if closes and m == 0:
                                last.then_inc(full[b], 1)
                    last.then_inc(slab_used, 1)
                    c.passed(stage(slab=1))
                    if between:
                        between(first + n)
                if stop:
                    c.passed({f"b{2 * half}": 1, f"b{2 * half + 1}": 1})

            def transpose_pair(i, source, base):
                b = 4 + i % 4
                wait(pe, drained[b], base[f"b{b}"] + i // 4)
                for a in range(2):
                    for m in range(HALVES):
                        k = 2 * i + a
                        last = pe.transpose(bank[b][:, (2 * a + m) * P:(2 * a + m + 1) * P],
                                            source(m)[:, k * P:(k + 1) * P], ident[:])
                last.then_inc(full[b], 1)

            def entry_panel(source, target, arrived):
                base = c.taken()

                def turn(i):
                    if i < SLABS:
                        arrived(i)
                        transpose_pair(i, source, base)

                for i in range(3):
                    turn(i)
                columns_panel(target, before=lambda i: pe.wait_ge(split_low, base["low"] + (i + 1)),
                              between=lambda i: turn(i + 3))
                c.passed(TRANSPOSE)

            def normalised(i):
                if i % 2 == 0:
                    pe.wait_ge(norm_ready, c["xn"] + HALVES * (i // 2 + 1))

            def attention(parts, products):
                base = c.taken()

                def step(j):
                    h = j - 2
                    if 0 <= h < TILES:
                        pe.wait_ge(prob_ready, base["prob"] + 2 * (h + 1))
                        for g, blocks in enumerate(parts(h)):
                            wait(pe, drained[4 + g], base[f"b{4 + g}"] + h)
                            for n, part in enumerate(blocks):
                                last = pe.transpose(bank[4 + g][:, n * P:(n + 1) * P], part, ident[:])
                            last.then_inc(full[4 + g], 1)
                    h = j - 3
                    if 0 <= h < TILES:
                        wait(pe, drained[7], base["b7"] + h)
                        terms = products(h, pT[h % 2])
                        for g in range(len(parts(h))):
                            pe.wait_ge(drained[4 + g], base[f"b{4 + g}"] + (h + 1))
                        for n, (v, prob, tokens) in enumerate(terms):
                            last = pe.matmul(bank[7][:, tokens], v, prob, start=(n == 0), stop=(n == len(terms) - 1))
                        last.then_inc(full[7], 1)

                return step

            def mem_attention(layer):
                def parts(h):
                    return [[mem_scores[:, h, m, kt * P:(kt + 1) * P] for m in range(HALVES)] for kt in range(2)]

                def products(h, slot):
                    return [(mem_v[:, layer, kt, h * P:(h + 1) * P], slot[:, kt * TOKENS:(kt + 1) * TOKENS],
                             slice(0, TOKENS)) for kt in range(2)]

                return attention(parts, products)

            def block_attention():
                def parts(h):
                    return [[scores[:, h, g, n * P:(n + 1) * P] for n in (0, 1, 2)] for g in range(GROUPS)]

                def products(h, slot):
                    terms = []
                    for g in range(GROUPS):
                        at, cols = g * 3 * P, slice(h * P, (h + 1) * P)
                        terms.append((values[:, g, 0, cols], slot[:, at:at + 2 * P], slice(0, TOKENS)))
                        terms.append((values[:, g, 1, cols], slot[:, at + 2 * P:at + 3 * P], slice(P, TOKENS)))
                    return terms

                return attention(parts, products)

            def mem_scores_of(layer):
                for h in range(TILES):
                    pe.wait_ge(drained[h], c[f"b{h}"])
                    wait(pe, drained[4 + h], c[f"b{4 + h}"])
                    for m in range(HALVES):
                        last = pe.matmul(bank[4 + h][:, m * MEM_TOKENS:(m + 1) * MEM_TOKENS],
                                         qk_r[:, h, m * P:(m + 1) * P], mem_kT[:, layer, h, :],
                                         start=True, stop=True)
                    last.then_inc(full[4 + h], 1)
                c.passed(SCORES)

            def group(between=None):
                columns_panel(xT, between=between)
                if between:
                    c.passed(adds)
                columns_panel(xT)
                rows_slabs(xT, 0, range(SLABS))
                for h in range(TILES):
                    pe.wait_ge(drained[h], c[f"b{h}"] - (1 if h < HALVES else 0))
                    wait(pe, drained[4 + h], c[f"b{4 + h}"])
                    q, k = qk_r[:, h, :], qk_r[:, TILES + h, :]
                    pe.matmul(bank[4 + h][:, 0:P], q[:, 0:P], k[:, 0:P], start=True, stop=True)
                    pe.matmul(bank[4 + h][:, P:3 * P], q[:, P:2 * P], k, start=True, stop=True) \
                        .then_inc(full[4 + h], 1)
                c.passed(SCORES)

            pe.wait_ge(consts, 3)
            entry_panel(lambda m: mem_rows[:, m, :], hT, lambda i: i % 2 == 0 and pe.wait_ge(mem_in[i // 2], 16))
            base = c.taken()

            def turn_x(i):
                if i == 0:
                    pe.wait_ge(x_in, 16 * PANELS)
                transpose_pair(i, lambda m: resid[:, m, :], base)

            rows_slabs(hT, 0, range(SLABS), before=turn_x)
            c.passed(TRANSPOSE)
            constants_base = c.taken()

            def constants(i):
                if i == 0:
                    pe.wait_ge(consts, 5)
                    for b in (4, 5, 6):
                        pe.wait_ge(drained[b], constants_base[f"b{b}"])
                    for g in (1, 2):
                        same = residues[:, g - 1, :]
                        pe.matmul(bank[3 + g][:, 0:P], same[:, 0:P], same[:, 0:P], start=True, stop=True)
                        pe.matmul(bank[3 + g][:, P:3 * P], same[:, P:2 * P], same[:, :], start=True, stop=True) \
                            .then_inc(full[3 + g], 1)
                    pe.wait_ge(rows_in, 16 * 8)
                    pe.transpose(bank[6][:, 0:N_VECS], vec_rows[0:N_VECS, :], ident[0:N_VECS, 0:N_VECS]) \
                        .then_inc(full[6], 1)
                if i in (0, 1):
                    pe.wait_ge(drained[7], constants_base["b7"] + i)
                    for j in range(4):
                        last = pe.transpose(bank[7][:, j * P:(j + 1) * P], ws_rows[:, 4 * i + j, :], ident[:])
                    last.then_inc(full[7], 1)

            columns_panel(hT, between=constants)
            c.passed(CONSTANTS)
            rows_slabs(hT, 0, range(SLABS))

            pe.wait_ge(split_low, c["low"])
            columns_panel(xT)
            mem_scores_of(0)
            pending, adds = mem_attention(0), ATTEND_MEM
            for b in range(HEADS // TILES):
                group(pending)
                with c.loop(pe, GROUPS - 1, GROUP):
                    group()
                for m in range(HALVES):
                    pe.wait_ge(drained[m], c[f"b{m}"])
                pending, adds = block_attention(), ATTEND

            for layer in range(DEPTH):
                if layer == 1:
                    entry_panel(lambda m: resid[:, m, :], xT, normalised)
                    c.passed(NORM)
                    mem_scores_of(1)
                    rows_slabs(xT, 0, range(SLABS), between=mem_attention(1))
                    c.passed(ATTEND_MEM)
                    rows_slabs(xT, 1, range(SLABS))
                    gates = c.taken()

                    def spatial(i):
                        if i == SPATIAL_STEPS[0]:
                            pe.wait_ge(norm_ready, gates["xn"] + HALVES)
                            pe.wait_ge(causal_ready, 1)
                        for n in range(2 * HALVES):
                            if SPATIAL_STEPS[n] == i:
                                half, m = n // 2, n % 2
                                pe.wait_ge(drained[4 + n], gates[f"b{4 + n}"])
                                for j in range(4):
                                    g = 4 * half + j
                                    last = pe.matmul(bank[4 + n][:, j * P:(j + 1) * P], wsT[:, g, :],
                                                     v_gate[m][:, g * P:(g + 1) * P], start=True, stop=True)
                                last.then_inc(full[4 + n], 1)

                    rows_slabs(xT, 0, range(SLABS), between=spatial)
                    c.passed(stage(xn=HALVES))
                    c.passed(GATES)
                    mix = c.taken()

                    def turn_mix(i, first=0):
                        if i in MIX_STEPS:
                            for m in range(HALVES):
                                pe.wait_ge(drained[4 + first + m], mix[f"b{4 + first + m}"])
                            transpose_pair(first + MIX_STEPS.index(i), lambda m: u[:, m, :], mix)

                    rows_slabs(xT, 1, range(SLABS), between=turn_mix)
                    pending, adds = (lambda i: turn_mix(i, 2)), TRANSPOSE_MIX
                    pe.wait_ge(split_low, mix["low"] + 2)
                pe.wait_ge(drained[7], c["b7"] if layer == 0 else gates["b7"])
                for half in range(2):
                    rows_slabs(hT, half, OUT_EARLY, stop=False, between=pending, first=half * len(OUT_EARLY))
                c.passed(adds)
                pe.wait_ge(drained[7], c["b7"])
                pe.wait_ge(split_low, c["low"])
                for half in range(2):
                    rows_slabs(hT, half, OUT_LATE, start=False)
                for half in range(2):
                    rows_slabs(hT, half, range(OUT_SLABS))
                c.passed(stage(stat=4 * HALVES))
                entry_panel(lambda m: resid[:, m, :], xT, normalised)
                c.passed(NORM)

                def rest(n):
                    with c.loop(pe, n, HIDDEN):
                        columns_panel(xT)
                        c.passed(besides(HIDDEN, COLUMNS))
                    with c.loop(pe, PANELS // 2, RESIDUAL):
                        def units(i):
                            if i == 0:
                                pe.wait_ge(split_low, c["low"] - TILES)
                            if i == SLABS - 2:
                                pe.wait_ge(split_low, c["low"])

                        for half in range(2):
                            rows_slabs(hT, half, range(SLABS), before=units)
                        c.passed(stage(stat=2 * HALVES))

                c.passed(besides(HIDDEN, COLUMNS))
                rest(PANELS - 1)
                with c.loop(pe, QUARTERS - 1, MLP_QUARTER):
                    rest(PANELS)
            assert c["slab"] == TOTAL_SLABS


_OUT = (1, TOKENS, D_MODEL)


def kernel(**inputs):
    import numpy as np
    import concourse.bacc as bacc
    from concourse.bass_utils import run_bass_kernel_spmd

    names = ["x", "mem", "w_in_a", "w_in_b", "w_s", "b_s", "vnorm_g", "vnorm_b", "w_mem_kv", "w_out",
             "ln1_g", "ln1_b", "w_ff1", "w_ff2", "ln2_g", "ln2_b"]
    nc = bacc.Bacc("TRN2", target_bir_lowering=False, num_devices=1)
    arrays, args = {}, []
    for name in names:
        a = np.ascontiguousarray(inputs[name])
        arrays[f"in_{name}"] = a
        args.append(nc.dram_tensor(f"in_{name}", a.shape, mybir.dt.from_np(a.dtype), kind="ExternalInput").ap())
    out = nc.dram_tensor("out_0", _OUT, F32, kind="ExternalOutput").ap()
    trunk(nc, *args, out)
    r = run_bass_kernel_spmd(nc, [arrays], core_ids=[0])
    return r.results[0]["out_0"]
```
